# Optimizing a Trainium2 kernel written in Bass

```python
import jax, jax.numpy as jnp
from jax import lax
import numpy as np

D_MODEL = 1024
BATCH = 1
SEQ = 512
DEPTH = 2
DEC_BATCH = 8
DEC_SEQ = 8
PAST_LEN = 2048
PAGE_SIZE = 128

N_MIXERS = 2
N_MLA_LAYERS = (DEPTH + 1) // 2
N_GLA_LAYERS = DEPTH // 2
D_FF = 2816
FFN_RESID = 0.5
EPS = 1e-6

MLA_HEADS = 8
MLA_Q_LORA = 384
MLA_KV_LORA = 256
MLA_NOPE = 128
MLA_ROPE = 64
MLA_V = 128
MLA_SCALE = (MLA_NOPE + MLA_ROPE) ** -0.5
ROPE_THETA = 10000.0
Q_BLOCK = 128

GLA_HEADS = 4
GLA_DK = D_MODEL // 2 // GLA_HEADS
GLA_DV = D_MODEL // GLA_HEADS
GLA_GATE_RANK = 16
GLA_GATE_NORM = 16.0
GLA_CHUNK = 64

kernel_name = 'hybrid_mla_gla_macaron_step'

def rmsnorm(x, g):
    xf = x.astype(jnp.float32)
    y = xf * lax.rsqrt(jnp.mean(xf * xf, axis=-1, keepdims=True) + EPS)
    return (y * g.astype(jnp.float32)).astype(x.dtype)

def ffn_half(h, g_pre, g_post, w_in, w_out):
    a = rmsnorm(h, g_pre) @ w_in
    gate, up = jnp.split(a, 2, axis=-1)
    return h + FFN_RESID * rmsnorm((jax.nn.silu(gate) * up) @ w_out, g_post)

def rope(x, pos):
    half = MLA_ROPE // 2
    inv = ROPE_THETA ** (-jnp.arange(half, dtype=jnp.float32) / half)
    ang = pos.astype(jnp.float32)[:, None] * inv[None, :]
    cos = jnp.cos(ang)[None, :, None, :]
    sin = jnp.sin(ang)[None, :, None, :]
    xf = x.astype(jnp.float32)
    x1, x2 = xf[..., :half], xf[..., half:]
    return jnp.concatenate([x1 * cos - x2 * sin, x2 * cos + x1 * sin], axis=-1).astype(x.dtype)

def mla_project(x, pos, w_down, g_q, w_uq, g_kv):
    B, S, _ = x.shape
    d = x @ w_down
    c_q = rmsnorm(d[..., :MLA_Q_LORA], g_q)
    c_kv = rmsnorm(d[..., MLA_Q_LORA:MLA_Q_LORA + MLA_KV_LORA], g_kv)
    k_pe = rope(d[..., MLA_Q_LORA + MLA_KV_LORA:][:, :, None, :], pos)[:, :, 0, :]
    q = (c_q @ w_uq).reshape(B, S, MLA_HEADS, MLA_NOPE + MLA_ROPE)
    q_nope = q[..., :MLA_NOPE]
    q_pe = rope(q[..., MLA_NOPE:], pos)
    return q_nope, q_pe, c_kv, k_pe

def mla_prompt(x, w_down, g_q, w_uq, g_kv, w_uk, w_uv, w_o):
    B, S, _ = x.shape
    pos = jnp.arange(S)
    q_nope, q_pe, c_kv, k_pe = mla_project(x, pos, w_down, g_q, w_uq, g_kv)
    k_nope = jnp.einsum('bsr,rhd->bshd', c_kv, w_uk)
    v = jnp.einsum('bsr,rhd->bshd', c_kv, w_uv)
    n_blk = S // Q_BLOCK
    qn_b = q_nope.reshape(B, n_blk, Q_BLOCK, MLA_HEADS, MLA_NOPE).swapaxes(0, 1)
    qp_b = q_pe.reshape(B, n_blk, Q_BLOCK, MLA_HEADS, MLA_ROPE).swapaxes(0, 1)
    key_pos = jnp.arange(S)

    def block(args):
        qn, qp, i = args
        s = (jnp.einsum('bqhd,bkhd->bhqk', qn, k_nope)
             + jnp.einsum('bqhr,bkr->bhqk', qp, k_pe)).astype(jnp.float32) * MLA_SCALE
        q_pos = i * Q_BLOCK + jnp.arange(Q_BLOCK)
        s = jnp.where(key_pos[None, :] <= q_pos[:, None], s, -jnp.inf)
        p = jax.nn.softmax(s, axis=-1).astype(v.dtype)
        return jnp.einsum('bhqk,bkhd->bqhd', p, v)

    o = lax.map(block, (qn_b, qp_b, jnp.arange(n_blk)))
    o = o.swapaxes(0, 1).reshape(B, S, MLA_HEADS * MLA_V)
    return o @ w_o, c_kv, k_pe

def mla_sample(x, cache_ckv, cache_kpe, page_table, w_down, g_q, w_uq, g_kv, w_uk, w_uv, w_o):
    B, T, _ = x.shape
    pos = PAST_LEN + jnp.arange(T)
    q_nope, q_pe, c_kv, k_pe = mla_project(x, pos, w_down, g_q, w_uq, g_kv)
    past_ckv = cache_ckv[page_table].reshape(B, -1, MLA_KV_LORA).astype(c_kv.dtype)
    past_kpe = cache_kpe[page_table].reshape(B, -1, MLA_ROPE).astype(k_pe.dtype)
    P = past_ckv.shape[1]
    all_ckv = jnp.concatenate([past_ckv, c_kv], axis=1)
    all_kpe = jnp.concatenate([past_kpe, k_pe], axis=1)
    q_lat = jnp.einsum('bthd,rhd->bthr', q_nope, w_uk)
    s = (jnp.einsum('bthr,bkr->bhtk', q_lat, all_ckv)
         + jnp.einsum('bthd,bkd->bhtk', q_pe, all_kpe)).astype(jnp.float32) * MLA_SCALE
    key_idx = jnp.arange(P + T)
    q_idx = P + jnp.arange(T)
    s = jnp.where(key_idx[None, :] <= q_idx[:, None], s, -jnp.inf)
    p = jax.nn.softmax(s, axis=-1).astype(all_ckv.dtype)
    o_lat = jnp.einsum('bhtk,bkr->bthr', p, all_ckv)
    o = jnp.einsum('bthr,rhd->bthd', o_lat, w_uv).reshape(B, T, MLA_HEADS * MLA_V)
    return o @ w_o, c_kv, k_pe

def gla_project(x, w_in, w_gk1, w_gk2, b_gk):
    B, S, _ = x.shape
    hk, hv = GLA_HEADS * GLA_DK, GLA_HEADS * GLA_DV
    p = x @ w_in
    q, k, v, og = jnp.split(p, [hk, 2 * hk, 2 * hk + hv], axis=-1)
    q = q.reshape(B, S, GLA_HEADS, GLA_DK) * GLA_DK ** -0.5
    k = k.reshape(B, S, GLA_HEADS, GLA_DK)
    v = v.reshape(B, S, GLA_HEADS, GLA_DV)
    gk = jax.nn.log_sigmoid(((x @ w_gk1) @ w_gk2 + b_gk).astype(jnp.float32)) / GLA_GATE_NORM
    gk = gk.reshape(B, S, GLA_HEADS, GLA_DK)
    return q, k, v, gk, og

def gla_chunk(state, q, k, v, g):
    qf, kf, vf = q.astype(jnp.float32), k.astype(jnp.float32), v.astype(jnp.float32)
    G = jnp.cumsum(g, axis=1)
    C = q.shape[1]
    causal = jnp.tril(jnp.ones((C, C), dtype=bool))
    diff = G[:, :, None] - G[:, None, :]
    decay = jnp.exp(jnp.where(causal[None, :, :, None, None], diff, -jnp.inf))
    attn = jnp.sum(qf[:, :, None] * kf[:, None, :] * decay, axis=-1)
    o = (jnp.einsum('bthk,bhkv->bthv', qf * jnp.exp(G), state)
         + jnp.einsum('btsh,bshv->bthv', attn, vf))
    g_last = G[:, -1]
    new_state = (jnp.exp(g_last)[..., None] * state
                 + jnp.einsum('bshk,bshv->bhkv', kf * jnp.exp(g_last[:, None] - G), vf))
    return new_state, o

def gla_output(o, og, g_norm, w_o):
    B, S = o.shape[:2]
    og = og.reshape(B, S, GLA_HEADS, GLA_DV)
    o = rmsnorm(o.astype(og.dtype), g_norm) * jax.nn.silu(og)
    return o.reshape(B, S, GLA_HEADS * GLA_DV) @ w_o

def gla_prompt(x, w_in, w_gk1, w_gk2, b_gk, g_norm, w_o):
    B, S, _ = x.shape
    q, k, v, gk, og = gla_project(x, w_in, w_gk1, w_gk2, b_gk)
    n = S // GLA_CHUNK

    def to_chunks(a):
        return a.reshape(B, n, GLA_CHUNK, *a.shape[2:]).swapaxes(0, 1)

    s0 = jnp.zeros((B, GLA_HEADS, GLA_DK, GLA_DV), jnp.float32)

    def step(state, inp):
        return gla_chunk(state, *inp)

    s_fin, o = lax.scan(step, s0, (to_chunks(q), to_chunks(k), to_chunks(v), to_chunks(gk)))
    o = o.swapaxes(0, 1).reshape(B, S, GLA_HEADS, GLA_DV)
    return gla_output(o, og, g_norm, w_o), s_fin

def gla_sample(x, state, w_in, w_gk1, w_gk2, b_gk, g_norm, w_o):
    q, k, v, gk, og = gla_project(x, w_in, w_gk1, w_gk2, b_gk)
    s_new, o = gla_chunk(state.astype(jnp.float32), q, k, v, gk)
    return gla_output(o, og, g_norm, w_o), s_new

def setup_inputs(seed: int = 0) -> dict:
    key = jax.random.key(seed)
    ks = jax.random.split(key, 24)
    n_pages = PAST_LEN // PAGE_SIZE
    n_pool = (DEC_BATCH * n_pages * 5) // 4

    def w(k, shape, fan_in):
        return jax.random.normal(k, shape, jnp.float32) * fan_in ** -0.5

    def gain(k, shape):
        return 1.0 + 0.02 * jax.random.normal(k, shape, jnp.float32)

    return {
        'x_prompt': jax.random.normal(ks[0], (BATCH, SEQ, D_MODEL), jnp.float32),
        'x_sample': jax.random.normal(ks[1], (DEC_BATCH, DEC_SEQ, D_MODEL), jnp.float32),
        'cache_ckv': jax.random.normal(ks[2], (N_MLA_LAYERS, n_pool, PAGE_SIZE, MLA_KV_LORA), jnp.float32),
        'cache_kpe': jax.random.normal(ks[3], (N_MLA_LAYERS, n_pool, PAGE_SIZE, MLA_ROPE), jnp.float32),
        'state_gla': 0.5 * jax.random.normal(ks[4], (N_GLA_LAYERS, DEC_BATCH, GLA_HEADS, GLA_DK, GLA_DV), jnp.float32),
        'page_table': jax.random.permutation(ks[5], n_pool)[:DEC_BATCH * n_pages].reshape(DEC_BATCH, n_pages).astype(jnp.int32),
        'norm_g': gain(ks[6], (DEPTH, 6, D_MODEL)),
        'ffn_w_in': w(ks[7], (DEPTH, 2, D_MODEL, 2 * D_FF), D_MODEL),
        'ffn_w_out': w(ks[8], (DEPTH, 2, D_FF, D_MODEL), D_FF),
        'mla_w_down': w(ks[9], (N_MLA_LAYERS, D_MODEL, MLA_Q_LORA + MLA_KV_LORA + MLA_ROPE), D_MODEL),
        'mla_g_q': gain(ks[10], (N_MLA_LAYERS, MLA_Q_LORA)),
        'mla_w_uq': w(ks[11], (N_MLA_LAYERS, MLA_Q_LORA, MLA_HEADS * (MLA_NOPE + MLA_ROPE)), MLA_Q_LORA),
        'mla_g_kv': gain(ks[12], (N_MLA_LAYERS, MLA_KV_LORA)),
        'mla_w_uk': w(ks[13], (N_MLA_LAYERS, MLA_KV_LORA, MLA_HEADS, MLA_NOPE), MLA_KV_LORA),
        'mla_w_uv': w(ks[14], (N_MLA_LAYERS, MLA_KV_LORA, MLA_HEADS, MLA_V), MLA_KV_LORA),
        'mla_w_o': w(ks[15], (N_MLA_LAYERS, MLA_HEADS * MLA_V, D_MODEL), MLA_HEADS * MLA_V),
        'gla_w_in': w(ks[16], (N_GLA_LAYERS, D_MODEL, 2 * GLA_HEADS * GLA_DK + 2 * GLA_HEADS * GLA_DV), D_MODEL),
        'gla_w_gk1': w(ks[17], (N_GLA_LAYERS, D_MODEL, GLA_GATE_RANK), D_MODEL),
        'gla_w_gk2': w(ks[18], (N_GLA_LAYERS, GLA_GATE_RANK, GLA_HEADS * GLA_DK), GLA_GATE_RANK),
        'gla_b_gk': 0.1 * jax.random.normal(ks[19], (N_GLA_LAYERS, GLA_HEADS * GLA_DK), jnp.float32),
        'gla_g_norm': gain(ks[20], (N_GLA_LAYERS, GLA_DV)),
        'gla_w_o': w(ks[21], (N_GLA_LAYERS, GLA_HEADS * GLA_DV, D_MODEL), GLA_HEADS * GLA_DV),
    }

def reference(x_prompt, x_sample, cache_ckv, cache_kpe, state_gla, page_table,
              norm_g, ffn_w_in, ffn_w_out,
              mla_w_down, mla_g_q, mla_w_uq, mla_g_kv, mla_w_uk, mla_w_uv, mla_w_o,
              gla_w_in, gla_w_gk1, gla_w_gk2, gla_b_gk, gla_g_norm, gla_w_o):
    yp, ys = x_prompt, x_sample
    ckv_p, kpe_p, ckv_s, kpe_s, st_p, st_s = [], [], [], [], [], []
    for i in range(DEPTH):
        g = norm_g[i]
        yp = ffn_half(yp, g[0], g[1], ffn_w_in[i, 0], ffn_w_out[i, 0])
        ys = ffn_half(ys, g[0], g[1], ffn_w_in[i, 0], ffn_w_out[i, 0])
        j = i // N_MIXERS
        if i % N_MIXERS == 0:
            mla_w = (mla_w_down[j], mla_g_q[j], mla_w_uq[j], mla_g_kv[j], mla_w_uk[j], mla_w_uv[j], mla_w_o[j])
            mp, c_p, k_p = mla_prompt(rmsnorm(yp, g[2]), *mla_w)
            ms, c_s, k_s = mla_sample(rmsnorm(ys, g[2]), cache_ckv[j], cache_kpe[j], page_table, *mla_w)
            ckv_p.append(c_p)
            kpe_p.append(k_p)
            ckv_s.append(c_s)
            kpe_s.append(k_s)
        else:
            gla_w = (gla_w_in[j], gla_w_gk1[j], gla_w_gk2[j], gla_b_gk[j], gla_g_norm[j], gla_w_o[j])
            mp, s_p = gla_prompt(rmsnorm(yp, g[2]), *gla_w)
            ms, s_s = gla_sample(rmsnorm(ys, g[2]), state_gla[j], *gla_w)
            st_p.append(s_p)
            st_s.append(s_s)
        yp = yp + rmsnorm(mp, g[3])
        ys = ys + rmsnorm(ms, g[3])
        yp = ffn_half(yp, g[4], g[5], ffn_w_in[i, 1], ffn_w_out[i, 1])
        ys = ffn_half(ys, g[4], g[5], ffn_w_in[i, 1], ffn_w_out[i, 1])
    new_ckv_prompt = jnp.stack(ckv_p, axis=0)
    new_kpe_prompt = jnp.stack(kpe_p, axis=0)
    new_ckv_sample = jnp.stack(ckv_s, axis=0)
    new_kpe_sample = jnp.stack(kpe_s, axis=0)
    new_state_prompt = jnp.stack(st_p, axis=0)
    new_state_sample = jnp.stack(st_s, axis=0)
    return (yp, ys, new_ckv_prompt, new_kpe_prompt, new_ckv_sample, new_kpe_sample, new_state_prompt, new_state_sample)


_drawn_inputs = setup_inputs


def setup_inputs(seed=0):
    import zlib

    import numpy as np

    out = dict(_drawn_inputs(seed))
    spreads = {}
    factors = {'mla_g_q': 2.794, 'gla_g_norm': 5.458}
    for name, (base, spread) in spreads.items():
        noise = np.random.default_rng([zlib.crc32(name.encode()), seed]).standard_normal(out[name].shape)
        drawn = base * np.exp(spread * noise) if base else spread * noise
        out[name] = __import__('jax').numpy.asarray(drawn.astype(out[name].dtype))
    for name, factor in factors.items():
        out[name] = (out[name] * factor).astype(out[name].dtype)
    return out
```

```python
from contextlib import ExitStack

import numpy as np

import concourse.bass as bass
from concourse import mybir

F32 = mybir.dt.float32
F32R = mybir.dt.float32r
ALU = mybir.AluOpType
ACT = mybir.ActivationFunctionType
AX = mybir.AxisListType

P = 128
D_MODEL, SEQ, DEC_BATCH, DEC_SEQ = 1024, 512, 8, 8
D_FF = 2816
EPS = 1e-6
FFN_RESID = 0.5
DT = D_MODEL // P
FT = D_FF // P
TOK = SEQ + DEC_BATCH * DEC_SEQ
HALF = TOK // 2
SLOTS = 3
SLOT_W = 8 * P
OUT_SPLIT = (8, 7, 7)
RING = 6

HEADS, NOPE, ROPE, VD = 8, 128, 64, 128
Q_LORA, KV_LORA = 384, 256
QT, KT = Q_LORA // P, KV_LORA // P
N_POOL, PAGE, PAST = 160, 128, 2048
PAGES = PAST // PAGE
MLA_SCALE = (NOPE + ROPE) ** -0.5
NEW = DEC_BATCH * DEC_SEQ
QR = HEADS * DEC_SEQ
QB = SEQ // P
ATT = HEADS * QB
MLA_IN = QT + KT + 1
MLA_BLOCKS = MLA_IN + HEADS + 2 + 2 + DT
MLA_UNITS = 2 * MLA_IN + 4 + 4 * HEADS + HEADS + 2 * QB + KT + 2 * DT
LOOK = 4
S_BANK = (0, 1, 6, 7)
PAIRS = DEC_BATCH // 2
GROUPS = PAGES // 4
SP_PAGES = 2
KEYS = 4 * PAGE

GH, DK, DV = 4, 128, 256
GATE_RANK, GATE_NORM = 16, 16.0
GATE_ONE = 32
GLA_IN = 1 + 2 * GH + 2 * DT
TT = 5
GLA_BLOCKS = GLA_IN + DT
LEVELS = 7
GLA_UNITS = 2 * GLA_IN + 4 * TT + TT + GH * (LEVELS + 1 + 4) + 2 * GH + 2 * DT
GLA_STORES = 1
STAGES = ["ffn", "mla", "ffn", "ffn", "gla", "ffn"]
PRE_GAIN = [0, 2, 4, 6, 8, 10]
POST_GAIN = [1, 3, 5, 7, 9, 11]


def hybrid_step(nc, io, stages=STAGES):
    pre_gain = PRE_GAIN
    post_gain = [None] + POST_GAIN
    with ExitStack() as ctx:
        def sem(name):
            return ctx.enter_context(nc.semaphore(name))

        at = [(nc.sbuf_base + 63) // 64 * 64]

        def sb(name, shape, dt=F32, offset=None):
            if offset is None:
                offset = at[0]
                at[0] += (int(np.prod(shape[1:])) * 4 + 31) // 32 * 32
            return nc.alloc_sbuf_tensor_at(name, shape, dt, offset=offset)

        psum = ctx.enter_context(nc.psum_tensor("psum", [P, 8, 512], F32))
        bank = [psum[:, i, :] for i in range(8)]

        h = sb("h", [P, DT, TOK])
        x_at = at[0]
        x_hi = sb("x_hi", [P, DT, TOK], F32R)
        x_lo = sb("x_lo", [P, DT, TOK], F32R)
        g_at = at[0]
        gu_hi = sb("gu_hi", [P, FT, TOK], F32R)
        gu_lo = sb("gu_lo", [P, FT, TOK], F32R)
        raw = [sb(f"raw{i}", [P, SLOT_W]) for i in range(SLOTS)]
        w_hi = [sb(f"w_hi{i}", [P, SLOT_W], F32R) for i in range(SLOTS)]
        w_lo = [sb(f"w_lo{i}", [P, SLOT_W], F32R) for i in range(SLOTS)]
        r_at = at[0]
        r_pre = sb("r_pre", [P, TOK])
        acc = sb("acc", [P, TOK])
        work_at = at[0]
        work = sb("work", [P, 4, HALF])
        sqp = sb("sqp", [P, 2, HALF])
        gains = sb("gains", [P, 12 * DT])
        gain_s = sb("gain_s", [P, 12 * DT])
        ones = sb("ones", [P, P])
        ident = sb("ident", [P, P])
        eps_d, eps_q, eps_kv, one_c = (sb(n, [P, 1]) for n in ("eps_d", "eps_q", "eps_kv", "one_c"))
        tail_at = at[0]
        y_ffn = sb("y_ffn", [P, DT, TOK], offset=x_at + DT * TOK * 4)
        y_mix = sb("y_mix", [P, DT, TOK], offset=g_at)

        W4 = TOK * 4
        qn = sb("qn", [P, HEADS, TOK], offset=g_at)
        qpe = sb("qpe", [ROPE, HEADS, TOK], offset=g_at + 8 * W4)
        down = sb("down", [P, MLA_IN, TOK], offset=g_at + 16 * W4)
        kn = sb("kn", [P, HEADS, SEQ], offset=g_at + 16 * W4)
        v_at = g_at + 16 * W4 + HEADS * SEQ * 4
        cq_hi = sb("cq_hi", [P, QT, TOK], F32R, offset=v_at)
        cq_lo = sb("cq_lo", [P, QT, TOK], F32R, offset=v_at + QT * W4)
        vp = sb("vp", [P, QB, HEADS * VD], offset=v_at)
        kv_at = v_at + QB * HEADS * VD * 4
        kv_hi = sb("kv_hi", [P, KT, TOK], F32R, offset=kv_at)
        kv_lo = sb("kv_lo", [P, KT, TOK], F32R, offset=kv_at + KT * W4)
        ckv = sb("ckv", [P, KT, TOK], offset=kv_at + 2 * KT * W4)
        kpe = sb("kpe", [ROPE, TOK], offset=kv_at + 3 * KT * W4)
        sc_at = kv_at + 3 * KT * W4 + W4
        down_sq = sb("down_sq", [P, QT + KT, TOK], offset=sc_at)
        uk_t = sb("uk_t", [P, HEADS, KV_LORA], offset=sc_at)
        pt = [sb(f"pt{i}", [P, QB, SEQ], offset=o) for i, o in enumerate((sc_at, kv_at))]
        q_lat = sb("q_lat", [P, KT, DEC_BATCH, QR], offset=sc_at + 8192)
        assert sc_at + 8192 + KT * DEC_BATCH * QR * 4 <= g_at + 2 * FT * W4
        q_pes = sb("q_pes", [ROPE, DEC_BATCH, QR], offset=tail_at)
        rope_tab = sb("rope_tab", [P, TOK], offset=tail_at + 2048)
        mask = sb("mask", [P, P + DEC_SEQ], offset=tail_at + 2048 + W4)
        st_at = tail_at + 2048 + W4 + (P + DEC_SEQ) * 4
        soft = sb("soft", [P, 8, ATT + PAIRS], offset=work_at + 16 * HALF)
        mla_g = sb("mla_g", [P, QT + KT], offset=st_at)
        table = sb("table", [1, DEC_BATCH * PAGES], mybir.dt.int32, offset=st_at + 32)
        assert st_at + 32 + 4 * DEC_BATCH * PAGES <= nc.sbuf_usable_end, (st_at, nc.sbuf_usable_end)
        prob = sb("prob", [P, LOOK, SEQ], offset=r_at)
        mx = sb("mx", [P, PAIRS, GROUPS + 1], offset=r_at + LOOK * SEQ * 4)
        sums = sb("sums", [P, PAIRS, GROUPS + 1], offset=r_at + LOOK * SEQ * 4 + 96)
        r_q = acc
        r_kv = sb("r_kv", [P, TOK], offset=work_at + 16 * HALF)
        C_W = PAGES * (KV_LORA + ROPE) * 4
        cache = [sb(f"cache{i}", [P, PAGES, KV_LORA + ROPE], offset=g_at + i * C_W) for i in range(SLOTS)]
        ct_at = g_at + SLOTS * C_W
        c_t = [sb(f"c_t{i}", [P, 3, KEYS], offset=ct_at + i * 12 * KEYS) for i in range(2)]
        uv_f = sb("uv_f", [P, KT, HEADS * VD], offset=ct_at)
        ol_at = ct_at + 24 * KEYS
        o_q = sb("o_q", [P, PAIRS, KV_LORA], offset=ol_at)
        o_lat = sb("o_lat", [P, KT, DEC_BATCH, QR], offset=ct_at + KT * HEADS * VD * 4)
        p_new = sb("p_new", [P, DEC_SEQ], offset=ol_at + 4096)
        p_new_t = sb("p_new_t", [DEC_SEQ, P], offset=ol_at + 4096 + 32)
        assert ol_at + 4096 + 32 + 4 * P <= kv_at + 2 * KT * W4
        p_s = sb("p_s", [P, GROUPS, KEYS], offset=sc_at)
        rows = sb("rows", [DEC_SEQ, 2, KV_LORA], offset=sc_at + 8192 + 4096)
        pt_s = sb("pt_s", [P, PAGES, P], offset=r_at)
        assert PAGES * P * 4 <= 32 * HALF


        qk = sb("qk", [P, 2 * GH, TOK], offset=g_at)
        cum = sb("cum", [P, GH, TOK], offset=g_at + 8 * W4)
        kd = sb("kd", [P, GH, TOK], offset=g_at + 12 * W4)
        att_p = sb("att_p", [P, GH, SEQ], offset=g_at + 12 * W4)
        att_s = sb("att_s", [NEW, GH, NEW], offset=g_at + 12 * W4 + GH * SEQ * 4)
        vt_f = sb("vt_f", [P, DT, TOK], offset=g_at + 16 * W4)
        o_t = sb("o_t", [P, DT, TOK], offset=g_at + 16 * W4)
        og = sb("og", [P, DT, TOK], offset=g_at + 24 * W4)
        qg = sb("qg", [P, GH, TOK], offset=g_at + 32 * W4)
        gk_at = g_at + 36 * W4
        gate = sb("gate", [P, TT, GH * DK], offset=gk_at)
        kd_t = sb("kd_t", [P, TT, GH * DK], offset=gk_at)
        o_sq = sb("o_sq", [P, DT, TOK], offset=g_at + 32 * W4)
        s_at = gk_at + TT * GH * DK * 4
        xl = [sb(f"xl{i}", [P, TOK], offset=s_at + i * W4) for i in range(3)]
        state = [sb(f"state{i}", [P, GH, DV], offset=s_at + i * GH * DV * 4) for i in range(2)]
        assert s_at + 2 * GH * DV * 4 <= g_at + 2 * FT * W4
        v_t = sb("v_t", [P, TT, GH * DV], offset=x_at)
        k_own = sb("k_own", [NEW, GH, DEC_BATCH, DK], offset=x_at + TT * GH * DV * 4)
        assert TT * GH * DV + GH * DEC_BATCH * DK <= 2 * DT * TOK
        SS = 6
        st_s = [sb(f"st_s{i}", [P, GH, DV], offset=g_at + i * GH * DV * 4) for i in range(SS)]
        o_r = sb("o_r", [P, GH, TOK], offset=g_at + 12 * W4)
        z_t = sb("z_t", [ROPE, TOK], offset=work_at + 16 * HALF)
        gk2 = sb("gk2", [GATE_ONE + 1, GH * DK], offset=r_at + W4)
        zc = sb("zc", [P, 2, GH * DK], offset=work_at)
        masked = sb("masked", [P, 2, SEQ], offset=work_at)
        masked_s = sb("masked_s", [NEW, 2, NEW], offset=work_at + 8 * SEQ)
        zmin = sb("zmin", [P, TT, GH * DK], offset=g_at + 24 * W4)
        lmask = sb("lmask", [P, LEVELS + 1, P], offset=tail_at)
        tri = sb("tri", [P, P + NEW], offset=tail_at + (LEVELS + 1) * P * 4)
        gc_at = tail_at + (LEVELS + 1) * P * 4 + (P + NEW) * 4
        glast = sb("glast", [P, GH, QB + DEC_BATCH], offset=gc_at)
        g_norm = sb("g_norm", [P, DV // P + DEC_BATCH], offset=gc_at + 192)
        eps_v = sb("eps_v", [P, 1], offset=gc_at + 192 + 64)
        assert gc_at + 192 + 96 <= nc.sbuf_usable_end, (gc_at, nc.sbuf_usable_end)

        s_h_in, s_const, s_gain = sem("s_h_in"), sem("s_const"), sem("s_gain")
        s_raw = [sem(f"s_raw{i}") for i in range(SLOTS)]
        s_hi, s_lo = sem("s_hi"), sem("s_lo")
        s_used = sem("s_used")
        s_unit, s_evicted = sem("s_unit"), sem("s_evicted")
        s_silu, s_gu, s_guhi, s_gulo = sem("s_silu"), sem("s_gu"), sem("s_guhi"), sem("s_gulo")
        s_sq, s_acc = sem("s_sq"), sem("s_acc")
        s_stat, s_root = sem("s_stat"), sem("s_root")
        s_rst, s_rpre = sem("s_rst"), sem("s_rpre")
        s_yn, s_hnew = sem("s_yn"), sem("s_hnew")
        s_xhi, s_xlo = sem("s_xhi"), sem("s_xlo")
        s_hsq, s_hacc = sem("s_hsq"), sem("s_hacc")
        s_out = sem("s_out")
        s_mla_c, s_ukt, s_uvf = sem("s_mla_c"), sem("s_ukt"), sem("s_uvf")
        s_dsq, s_mroot, s_mg = sem("s_dsq"), sem("s_mroot"), sem("s_mg")
        s_cq, s_cqhi, s_cqlo = sem("s_cq"), sem("s_cqhi"), sem("s_cqlo")
        s_ckv, s_kvhi, s_kvlo = sem("s_ckv"), sem("s_kvhi"), sem("s_kvlo")
        s_kpe, s_rt, s_rope, s_qpes = sem("s_kpe"), sem("s_rt"), sem("s_rope"), sem("s_qpes")
        s_s, s_msk, s_max, s_neg = sem("s_s"), sem("s_msk"), sem("s_max"), sem("s_neg")
        s_exp, s_rec, s_pn, s_t, s_pt = sem("s_exp"), sem("s_rec"), sem("s_pn"), sem("s_t"), sem("s_pt")
        s_o, s_ohi, s_olo = sem("s_o"), sem("s_ohi"), sem("s_olo")
        s_table = sem("s_table")
        s_cache = [[sem(f"s_cache{i}_{g}") for g in range(GROUPS)] for i in range(SLOTS)]
        s_cache_p = [[sem(f"s_cache_p{i}_{g}") for g in range(GROUPS)] for i in range(SLOTS)]
        s_tr, s_ctv, s_cta, s_score, s_snew = (sem(x) for x in ("s_tr", "s_ctv", "s_cta", "s_score", "s_snew"))
        s_mxs, s_negs, s_exps, s_recs = (sem(x) for x in ("s_mxs", "s_negs", "s_exps", "s_recs"))
        s_fill, s_fe, s_fa, s_pv, s_ole, s_so = (sem(x) for x in ("s_fill", "s_fe", "s_fa", "s_pv", "s_ole", "s_so"))
        g_const, g_gain = sem("g_const"), sem("g_gain")
        g_abs, g_ln, g_gate = sem("g_abs"), sem("g_ln"), sem("g_gate")
        g_eg, g_qg, g_last, g_kd = sem("g_eg"), sem("g_qg"), sem("g_last"), sem("g_kd")
        g_kdif, g_kexp = sem("g_kdif"), sem("g_kexp")
        g_dif, g_exp, g_xq, g_xk = sem("g_dif"), sem("g_exp"), sem("g_xq"), sem("g_xk")
        g_att, g_att_s = sem("g_att"), sem("g_att_s")
        g_silu, g_own = sem("g_silu"), sem("g_own")
        g_o, g_oe, g_s, g_se = sem("g_o"), sem("g_oe"), sem("g_s"), sem("g_se")
        g_so, g_soe, g_sn, g_sne = sem("g_so"), sem("g_soe"), sem("g_sn"), sem("g_sne")
        g_load = [sem(f"g_load{i}") for i in range(SS)]
        g_store = [sem(f"g_store{i}") for i in range(SS)]
        g_osq, g_root, g_rec, g_on, g_og = sem("g_osq"), sem("g_root"), sem("g_rec"), sem("g_on"), sem("g_og")
        g_ohi, g_olo = sem("g_ohi"), sem("g_olo")

        H = [slice(0, HALF), slice(HALF, TOK)]

        FB, FO = 2 * FT, DT * len(OUT_SPLIT)
        n_st = len(stages)
        n_blocks = {"ffn": FB + FO, "mla": MLA_BLOCKS, "gla": GLA_BLOCKS}
        n_units = {"ffn": 4 * FT + 2 * DT, "mla": MLA_UNITS, "gla": GLA_UNITS}
        first_block = [sum(n_blocks[k] for k in stages[:i]) for i in range(n_st + 1)]
        first_unit = [sum(n_units[k] for k in stages[:i]) for i in range(n_st + 1)]
        ffn_no = [sum(k == "ffn" for k in stages[:i]) for i in range(n_st)]
        stat_pre = [4 * b for b in range(n_st + 1)]
        stat_post = [None] + [4 * b - 2 for b in range(1, n_st + 1)]

        def pair_unit(j, hf):
            return 2 * hf + j if j < 2 else 2 * j + hf

        M_SUM = 2 * MLA_IN
        M_Q = M_SUM + 4
        M_K = M_Q + 4 * HEADS
        M_V = M_K + HEADS
        M_L = M_V + 2 * QB
        M_O = M_L + KT
        mla_used = ([3, 4] + [2 * j + 2 for j in range(2, MLA_IN)] + [M_Q + 4 * i + 4 for i in range(HEADS)]
                    + [M_K + 4, M_K + 8] + [M_V + 4, M_V + 8])

        g_plan = []
        spread = [("lev", hd, lv) for hd in range(GH) for lv in range(LEVELS + 1)]
        for j in range(2, GLA_IN):
            g_plan.append(("in", j, 0))
            if j == 2:
                g_plan += [("gate", t, 0) for t in range(TT)]
            if j == 5:
                g_plan += [("cum", hd, 0) for hd in range(GH + 1)]
            if j == 11:
                g_plan += [("kt", t, 0) for t in range(TT)]
            while j >= 12 and spread and (j + 1 - 12) * (GH * (LEVELS + 1)) > (GH * (LEVELS + 1) - len(spread)) * (GLA_IN - 12):
                kind, hd, lv = spread.pop(0)
                g_plan.append((kind, hd, lv))
                if lv >= 4:
                    g_plan.append(("levs", hd, lv))
        g_plan += [("vt", t, c) for t in range(TT) for c in range(2)]
        assert not spread
        g_unit, u = [], 4
        for kind, _, _ in g_plan:
            g_unit.append(u)
            u += 2 if kind == "in" else 1
        G_SUM = u
        G_O = G_SUM + 2 * GH
        assert G_O + 2 * DT == GLA_UNITS, (G_O + 2 * DT, GLA_UNITS)
        gla_used = [3, 4] + [u + 2 for (kind, _, _), u in zip(g_plan, g_unit) if kind == "in"]
        N_X = GH * LEVELS
        lev_unit = [0] * N_X
        for (kind, hd, lv), un in zip(g_plan, g_unit):
            if kind in ("lev", "levs") and lv < LEVELS:
                lev_unit[LEVELS * hd + lv] = un

        def x_of(i):
            return i // LEVELS, i % LEVELS

        def halves(tile, lv):
            b = P >> (lv + 1)
            n = TOK if lv >= 4 else SEQ
            v = tile[:, 0:n].rearrange("p (j c) -> p j c", c=2 * b)
            return v[:, :, 0:b], v[:, :, b:2 * b], v[:, :, b - 1:b].to_broadcast([P, n // (2 * b), b])

        def rows_of(t):
            return P if t < QB else NEW

        def load_pages(eng, u0, landed, lo, hi):
            eng.wait_ge(s_table, 16)
            eng.wait_ge(s_o, HEADS)
            eng.wait_ge(s_evicted, u0 + M_O)
            eng.wait_ge(s_qpes, HEADS)
            for b in range(DEC_BATCH):
                if b >= SLOTS:
                    eng.wait_ge(s_pv, b - SLOTS + 1)
                for g in range(GROUPS):
                    with eng.Fori(lo, hi) as i:
                        page = eng.value_load(table[0:1, bass.ds(PAGES * b + 4 * g + i, 1)], min_val=0,
                                              max_val=N_POOL - 1)
                        eng.dma_start(cache[b % SLOTS][:, 4 * g + i, :],
                                      io["cache"][page]).then_inc(landed[b % SLOTS][g], 16)

        blk = ctx.enter_context(nc.Block())

        @blk.sync
        def _(sp):
            sp.dma_start(h[:, :, H[0]], io["x_t"][:, :, H[0]]).then_inc(s_h_in, 16)
            sp.dma_start(gains[:, :], io["gains"]).then_inc(s_const, 16)

            def load(n, src, slot, width):
                if not (isinstance(n, int) and n < SLOTS):
                    sp.wait_ge(s_lo, n - (SLOTS - 1))
                sp.dma_start(raw[slot][:, 0:width], src).then_inc(s_raw[slot], 16)

            def ffn(st):
                b0, f = first_block[st], ffn_no[st]
                w_in, w_out = io["ffn_in"], io["ffn_out"]
                for j in range(2):
                    load(b0 + j, w_in[f, j], (b0 + j) % SLOTS, SLOT_W)
                    if st == 0 and j == 0:
                        sp.dma_start(h[:, :, H[1]], io["x_t"][:, :, H[1]]).then_inc(s_h_in, 16)
                with sp.Fori(0, (FB - 2) // 6) as i:
                    for j in range(6):
                        load(b0 + 2 + 6 * i + j, w_in[f, 2 + 6 * i + j], (b0 + 2 + j) % SLOTS, SLOT_W)
                b1 = b0 + FB
                with sp.Fori(0, DT) as m:
                    k0 = 0
                    for c, nk in enumerate(OUT_SPLIT):
                        load(b1 + 3 * m + c, w_out[f, m, :, k0 * P:(k0 + nk) * P], (b1 + c) % SLOTS, nk * P)
                        k0 += nk

            def mla(st):
                n0, u0 = first_block[st], first_unit[st]
                srcs = [io["mla_down"][j] for j in range(MLA_IN)] + [io["mla_uq"][j] for j in range(HEADS)]
                srcs += [io["mla_uk"][j] for j in range(2)] + [io["mla_uv"][j] for j in range(2)]
                srcs += [io["mla_wo"][m] for m in range(DT)]

                def load_n(j):
                    load(n0 + j, srcs[j], (n0 + j) % SLOTS, srcs[j].shape[1])

                for j in range(MLA_IN):
                    load_n(j)
                sp.dma_start(rope_tab[:, :], io["rope_tab"]).then_inc(s_mla_c, 16)
                sp.dma_start(mask[:, :], io["mask"]).then_inc(s_mla_c, 16)
                sp.dma_start(mla_g[:, :], io["mla_g"]).then_inc(s_mla_c, 16)
                sp.dma_start(table[:, :], io["page_table"]).then_inc(s_table, 16)
                for j in range(MLA_IN, MLA_IN + HEADS):
                    load_n(j)
                sp.wait_ge(s_evicted, u0 + M_SUM + 4)
                sp.dma_start(uk_t[:, :, :], io["mla_uk_t"]).then_inc(s_ukt, 16)
                sp.wait_ge(s_ckv, KT)
                sp.dma_start(io["ckv_t"], ckv[:, :, :]).then_inc(s_out, 16)
                sp.wait_ge(s_kpe, 1)
                sp.dma_start(io["kpe_t"], kpe[:, :]).then_inc(s_out, 16)
                for j in range(MLA_IN + HEADS, MLA_IN + HEADS + 4 + SLOTS):
                    load_n(j)
                load_pages(sp, u0, s_cache, 0, SP_PAGES)
                sp.wait_ge(s_score, GROUPS * DEC_BATCH)
                sp.dma_start(uv_f[:, :, :], io["mla_uv_f"]).then_inc(s_uvf, 16)
                for j in range(MLA_BLOCKS - DT + SLOTS, MLA_BLOCKS):
                    load_n(j)

            def gla(st):
                n0 = first_block[st]
                sp.wait_ge(s_lo, n0)
                for dst, name in ((lmask, "lmask"), (tri, "tri"), (g_norm, "g_norm")):
                    sp.dma_start(dst[:, :] if name != "lmask" else dst[:, :, :], io[name]).then_inc(g_const, 16)

                def load_n(j):
                    src = io["gla_in"][j] if j < GLA_IN else io["gla_wo"][j - GLA_IN]
                    load(n0 + j, src, (n0 + j) % SLOTS, SLOT_W)

                for j in range(4):
                    load_n(j)
                sp.wait_ge(s_rpre, 2 * st + 2)
                sp.dma_start(gk2[:, :], io["gk2"]).then_inc(g_const, 16)
                for j in range(4, GLA_IN + SLOTS):
                    load_n(j)
                sp.wait_ge(g_att, GH * LEVELS)
                sp.wait_ge(g_att_s, 3 * GH)
                for b in range(SS):
                    sp.dma_start(st_s[b][:, :, :], io["state_gla"][b]).then_inc(g_load[b], 16)
                sp.wait_ge(g_se, GH * QB)
                sp.dma_start(io["state_p"], state[0][:, :, :]).then_inc(s_out, 16)
                for b in range(DEC_BATCH):
                    sp.wait_ge(g_sne, 2 * (b + 1))
                    sp.dma_start(io["state_s"][b], st_s[b % SS][:, :, :]).then_inc(g_store[b % SS], 16)
                    if b + SS < DEC_BATCH:
                        sp.wait_ge(g_store[b % SS], 16)
                        sp.dma_start(st_s[b % SS][:, :, :], io["state_gla"][b + SS]).then_inc(g_load[b % SS], 16)
                for i in range(SS):
                    sp.wait_ge(g_store[i], 32 if i + SS < DEC_BATCH else 16)
                for j in range(GLA_IN + SLOTS, GLA_BLOCKS):
                    load_n(j)

            sp.dma_start(ident[:, :], io["ident"]).then_inc(s_const, 16)
            for st, kind in enumerate(stages):
                {"ffn": ffn, "mla": mla, "gla": gla}[kind](st)
            sp.wait_ge(s_hnew, 2 * DT * n_st)
            sp.dma_start(io["y_t"], h[:, :, :]).then_inc(s_out, 16)
            sp.wait_ge(s_out, 16 * (1 + 2 * stages.count("mla") + GLA_STORES * stages.count("gla")))

        @blk.scalar
        def _(act):
            def split_hi(slot, landed, used=None):
                act.wait_ge(s_raw[slot], landed)
                if used is not None:
                    act.wait_ge(*used)
                act.activation(w_hi[slot][:, :], raw[slot][:, :], ACT.Copy).then_inc(s_hi, 1)

            def landed(n):
                return 16 * (n // SLOTS + 1)

            def root(count, dst, hf):
                act.wait_ge(s_stat, count)
                act.activation(dst, bank[6 + hf][:, 0:HALF], ACT.Sqrt, bias=eps_d[:, 0:1]).then_inc(s_root, 1)

            def chain(b, hf, ks=range(DT)):
                for k in ks:
                    c = 2 * DT * b + DT * hf + k
                    if b == 0:
                        act.wait_ge(s_h_in, 16 * (hf + 1))
                        act.wait_ge(s_gain, 2)
                    else:
                        act.wait_ge(s_hnew, c - 2 * DT + 1)
                    gk = pre_gain[b] * DT + k
                    act.activation(x_hi[:, k, H[hf]], h[:, k, H[hf]], ACT.Identity,
                                   scale=gain_s[:, gk:gk + 1]).then_inc(s_xhi, 1)
                    if c >= 2:
                        act.wait_ge(s_hacc, c - 1)
                    act.activation(sqp[:, c % 2, :], h[:, k, H[hf]], ACT.Square).then_inc(s_hsq, 1)

            def roots_pre(st):
                root(stat_pre[st] + 1, r_pre[:, H[0]], 0)
                root(stat_pre[st] + 2, r_pre[:, H[1]], 1)

            def silu(u, hf):
                act.wait_ge(s_evicted, u + 1)
                act.activation(work[:, hf, :], work[:, hf, :], ACT.Silu).then_inc(s_silu, 1)

            def gate_hi(n, i, hf):
                act.wait_ge(s_gu, n + 1)
                act.activation(gu_hi[:, i, H[hf]], work[:, 2 + hf, :], ACT.Copy).then_inc(s_guhi, 1)

            def square(y, m, hf, ev, acc_n=None):
                act.wait_ge(s_evicted, ev)
                if acc_n is not None:
                    act.wait_ge(s_acc, acc_n)
                act.activation(work[:, hf, :], y[:, m, H[hf]], ACT.Square).then_inc(s_sq, 1)

            def ffn(st):
                b0, u0, f = first_block[st], first_unit[st], ffn_no[st]
                q0 = 2 * FT * f
                roots_pre(st)
                silu(u0, 0)
                gate_hi(q0, 0, 0)
                split_hi((b0 + 3) % SLOTS, landed(b0 + 3), (s_unit, u0 + 3))
                silu(u0 + 2, 1)
                gate_hi(q0 + 1, 0, 1)
                with act.Fori(0, (FT - 1) // 3) as i:
                    for p in range(1, 4):
                        n = b0 + 2 * p + 2
                        split_hi(n % SLOTS, landed(n) + 32 * i, (s_unit, u0 + 4 * p + 12 * i))
                        for hf in range(2):
                            silu(u0 + 4 * p + hf + 12 * i, hf)
                        split_hi((n + 1) % SLOTS, landed(n + 1) + 32 * i, (s_unit, u0 + 4 * p + 2 + 12 * i))
                        for hf in range(2):
                            gate_hi(q0 + 2 * p + hf + 6 * i, p + 3 * i, hf)
                n0, v0 = b0 + FB, u0 + 4 * FT

                def split_out(m, c):
                    n = n0 + c + 2
                    used = (s_unit, v0 + 2 * m) if c == 0 else (s_used, 2 * DT * f + 2 * m + c)
                    split_hi(n % SLOTS, landed(n) + 16 * m, used)

                with act.Fori(0, DT - 1) as m:
                    for c in range(3):
                        split_out(m, c)
                    for hf in range(2):
                        square(y_ffn, m, hf, v0 + 2 * m + hf + 1)
                m, b = DT - 1, st + 1
                split_out(m, 0)
                square(y_ffn, m, 0, v0 + 2 * m + 1)
                root(stat_post[b] + 1, work[:, 2, :], 0)
                if b < n_st:
                    chain(b, 0, range(0, 4))
                    split_out(m, 1)
                    chain(b, 0, range(4, 8))
                    split_out(m, 2)
                square(y_ffn, m, 1, v0 + 2 * m + 2)
                root(stat_post[b] + 2, work[:, 3, :], 1)
                if b < n_st:
                    n = first_block[b] + 2
                    split_hi(n % SLOTS, landed(n), (s_unit, first_unit[b]))
                    chain(b, 1)

            def mix_out(st, n0, v0):
                with act.Fori(0, 2) as i:
                    for m in range(3):
                        n = n0 + m + 2
                        split_hi(n % SLOTS, landed(n) + 16 * i, (s_unit, v0 + 2 * m + 6 * i))
                        for hf in range(2):
                            square(y_mix, m + 3 * i, hf, v0 + 2 * m + hf + 1 + 6 * i)
                a0, b = 2 * DT * st, st + 1
                n = n0 + DT
                split_hi(n % SLOTS, landed(n), (s_unit, v0 + 12))
                square(y_mix, 6, 0, v0 + 13)
                square(y_mix, 7, 0, v0 + 14, a0 + 13)
                root(stat_post[b] + 1, work[:, 2, :], 0)
                chain(b, 0, range(0, 4))
                split_hi((n + 1) % SLOTS, landed(n + 1), (s_unit, v0 + 15))
                chain(b, 0, range(4, 8))
                square(y_mix, 6, 1, v0 + 15)
                square(y_mix, 7, 1, v0 + 16, a0 + 15)
                root(stat_post[b] + 2, work[:, 3, :], 1)
                split_hi((n + 2) % SLOTS, landed(n + 2), (s_unit, v0 + 16))
                chain(b, 1)

            def mla(st):
                n0, u0 = first_block[st], first_unit[st]

                def split_n(j):
                    split_hi((n0 + j) % SLOTS, landed(n0 + j), (s_unit, u0 + mla_used[j - 3]))

                roots_pre(st)
                for j in range(3, MLA_IN + 3):
                    split_n(j)
                for j in range(QT + KT):
                    act.wait_ge(s_evicted, u0 + pair_unit(j, 1) + 1)
                    act.activation(down_sq[:, j, :], down[:, j, :], ACT.Square).then_inc(s_dsq, 1)
                for j in range(2):
                    dst, eps = ((r_q, eps_q), (r_kv, eps_kv))[j]
                    for hf in range(2):
                        act.wait_ge(s_unit, u0 + M_SUM + 2 * j + hf + 1)
                        act.activation(dst[:, H[hf]], bank[(u0 + M_SUM + 2 * j + hf) % RING][:, 0:HALF], ACT.Sqrt,
                                       bias=eps[:, 0:1]).then_inc(s_mroot, 1)
                for j in range(QT):
                    act.wait_ge(s_cq, j + 1)
                    act.activation(cq_hi[:, j, :], down[:, j, :], ACT.Copy).then_inc(s_cqhi, 1)
                for j in range(KT):
                    act.wait_ge(s_ckv, j + 1)
                    act.activation(kv_hi[:, j, :], ckv[:, j, :], ACT.Copy).then_inc(s_kvhi, 1)
                for j in range(MLA_IN + 3, MLA_BLOCKS - DT + 2):
                    split_n(j)

                def out_hi(hd):
                    act.wait_ge(s_o, hd + 1)
                    act.activation(x_hi[:, hd, 0:SEQ], bank[4 + hd % 2], ACT.Copy).then_inc(s_ohi, 1)

                for w in range(ATT + 2):
                    if w < ATT:
                        n = (w % QB + 1) * P
                        act.wait_ge(s_neg, w + 1)
                        if w >= LOOK:
                            act.wait_ge(s_t, w - LOOK + 1)
                        else:
                            act.wait_ge(s_rope, 2 * HEADS + 1)
                        act.activation(prob[:, w % LOOK, 0:n], bank[S_BANK[w % LOOK]][:, 0:n], ACT.Exp,
                                       bias=soft[:, 1, w:w + 1], scale=MLA_SCALE,
                                       accum_out=soft[:, 2, w:w + 1]).then_inc(s_exp, 1)
                    if w >= 2:
                        v = w - 2
                        hd, i = v // QB, v % QB
                        act.wait_ge(s_t, v + 1)
                        if hd < 2 and i == 0:
                            act.wait_ge(s_evicted, u0 + M_O)
                        if hd >= 2 and i == 0:
                            act.wait_ge(s_o, hd - 1)
                        act.activation(pt[hd % 2][:, 0:i + 1, i * P:(i + 1) * P],
                                       bank[2 + v % 2][:, 0:(i + 1) * P].rearrange("p (k q) -> p k q", q=P),
                                       ACT.Copy).then_inc(s_pt, 1)
                    if w % QB == QB - 1 and w > QB:
                        out_hi(w // QB - 1)
                out_hi(HEADS - 1)

                def pages(x):
                    for j in (1, 2):
                        act.wait_ge(s_tr, 3 * x + j + 1)
                        if x >= 2 and j == 1:
                            act.wait_ge(s_score, x - 1)
                        r = P if j == 1 else ROPE
                        act.activation(c_t[x % 2][0:r, j, :], bank[4 + j][0:r, :], ACT.Copy).then_inc(s_cta, 1)

                for bp in range(PAIRS):
                    for x in range(2 * GROUPS * bp + (bp > 0), 2 * GROUPS * (bp + 1)):
                        pages(x)
                    w = ATT + bp
                    act.wait_ge(s_negs, bp + 1)
                    if bp > 0:
                        act.wait_ge(s_fill, 6 * bp)
                    for f in range(GROUPS):
                        act.activation(p_s[:, f, :], bank[f], ACT.Exp, bias=soft[:, 1, w:w + 1], scale=MLA_SCALE,
                                       accum_out=sums[:, bp, f:f + 1]).then_inc(s_exps, 1)
                    act.activation(p_new[:, :], p_new[:, :], ACT.Exp, bias=soft[:, 1, w:w + 1], scale=MLA_SCALE,
                                   accum_out=sums[:, bp, GROUPS:GROUPS + 1]).then_inc(s_exps, 1)
                    if bp + 1 < PAIRS:
                        pages(2 * GROUPS * (bp + 1))
                    for f in (1, 3):
                        act.wait_ge(s_fill, 6 * bp + 2 + f)
                        if bp > 0 and f == 1:
                            act.wait_ge(s_pv, 2 * bp)
                        act.activation(pt_s[:, 4 * f:4 * f + 4, :], bank[f].rearrange("p (g q) -> p g q", q=P),
                                       ACT.Copy).then_inc(s_fa, 1)
                act.wait_ge(s_so, 1)
                act.activation(x_hi[:, :, SEQ:TOK], bank[4].rearrange("p (h q) -> p h q", h=HEADS),
                               ACT.Copy).then_inc(s_ohi, 1)
                mix_out(st, n0 + MLA_BLOCKS - DT, u0 + M_O)

            def gla(st):
                n0, u0 = first_block[st], first_unit[st]

                def split_n(j):
                    split_hi((n0 + j) % SLOTS, landed(n0 + j), (s_unit, u0 + gla_used[j - 3]))

                def level_exp(i):
                    if i < N_X:
                        hd, lv = x_of(i)
                        n = TOK if lv >= 4 else SEQ
                        act.wait_ge(g_dif, 2 * (i + 1))
                        act.activation(xl[i % 3][:, 0:n], xl[i % 3][:, 0:n], ACT.Exp).then_inc(g_exp, 1)

                roots_pre(st)
                split_n(3)
                xi = 0
                for (kind, a, c), u in zip(g_plan, g_unit):
                    if kind == "in" and a + 2 < GLA_IN + 2:
                        split_n(a + 2)
                    if kind == "gate":
                        r = rows_of(a)
                        act.wait_ge(g_abs, a + 1)
                        act.activation(gate[0:r, a, :], gate[0:r, a, :], ACT.Exp, scale=-1.0).then_inc(g_eg, 1)
                    if kind == "gate" and a == TT - 1:
                        for t in range(TT):
                            r = rows_of(t)
                            act.wait_ge(g_eg, t + 1)
                            act.activation(gate[0:r, t, :], gate[0:r, t, :], ACT.Ln, bias=one_c[0:r, 0:1]).then_inc(g_ln, 1)
                    if kind == "cum" and a == GH:
                        act.wait_ge(s_evicted, u0 + u + 1)
                        for hd in range(GH):
                            act.activation(qg[:, hd, :], cum[:, hd, :], ACT.Exp).then_inc(g_eg, 1)
                        act.activation(glast[:, :, 0:QB],
                                       cum[:, :, 0:SEQ].rearrange("p h (c t) -> p h c t", t=P)[:, :, :, P - 1],
                                       ACT.Exp).then_inc(g_last, 1)
                        act.activation(glast[:, :, QB:],
                                       cum[:, :, SEQ:].rearrange("p h (c t) -> p h c t", t=DEC_SEQ)[:, :, :, DEC_SEQ - 1],
                                       ACT.Exp).then_inc(g_last, 1)
                    if kind == "in" and a == 9:
                        for hd in range(GH):
                            act.wait_ge(g_kdif, 2 * (hd + 1))
                            act.activation(kd[:, hd, :], kd[:, hd, :], ACT.Exp).then_inc(g_kexp, 1)
                    if kind == "kt" and a == TT - 1:
                        level_exp(0)
                        level_exp(1)
                    if kind == "lev" and c < LEVELS:
                        level_exp(xi + 2)
                        xi += 1
                for m in range(DT):
                    act.wait_ge(s_evicted, u0 + gla_used[GLA_IN - DT + m])
                    act.activation(og[:, m, :], og[:, m, :], ACT.Silu).then_inc(g_silu, 1)
                for m in range(DT):
                    act.wait_ge(g_soe, 1)
                    act.wait_ge(g_oe, GH * QB)
                    act.wait_ge(g_sne, 2 * DEC_BATCH)
                    act.activation(o_sq[:, m, :], o_t[:, m, :], ACT.Square).then_inc(g_osq, 1)
                for hd in range(GH):
                    for hf in range(2):
                        u = u0 + G_SUM + 2 * hd + hf
                        act.wait_ge(s_unit, u + 1)
                        act.activation(o_r[:, hd, H[hf]], bank[u % RING][:, 0:HALF], ACT.Sqrt,
                                       bias=eps_v[:, 0:1]).then_inc(g_root, 1)
                for m in range(DT):
                    act.wait_ge(g_og, m + 1)
                    act.activation(x_hi[:, m, :], o_t[:, m, :], ACT.Copy).then_inc(g_ohi, 1)
                mix_out(st, n0 + GLA_IN, u0 + G_O)

            split_hi(0, 16)
            split_hi(1, 16)
            chain(0, 0)
            split_hi(2, 16)
            chain(0, 1)
            for st, kind in enumerate(stages):
                {"ffn": ffn, "mla": mla, "gla": gla}[kind](st)

        @blk.gpsimd
        def _(pool):
            def split_lo(slot, n1):
                pool.wait_ge(s_hi, n1)
                pool.tensor_tensor(w_lo[slot][:, :], raw[slot][:, :], w_hi[slot][:, :].bitcast(F32),
                                   ALU.subtract).then_inc(s_lo, 1)

            def low(n):
                split_lo(n % SLOTS, n + 1)

            def hacc(b, hf, ks=range(DT)):
                for k in ks:
                    c = 2 * DT * b + DT * hf + k
                    pool.wait_ge(s_hsq, c + 1)
                    if k == 0:
                        if b > 0:
                            pool.wait_ge(s_rst, 2 * (b - 1) + hf + 1)
                        pool.tensor_copy(acc[:, H[hf]], sqp[:, c % 2, :]).then_inc(s_hacc, 1)
                    else:
                        pool.wait_ge(s_hacc, c)
                        pool.tensor_tensor(acc[:, H[hf]], acc[:, H[hf]], sqp[:, c % 2, :], ALU.add).then_inc(s_hacc, 1)

            def ffn(st):
                b0 = first_block[st]
                low(b0 + 3)
                with pool.Fori(0, (FT - 1) // 3) as i:
                    for j in range(6):
                        n = b0 + 4 + j
                        split_lo(n % SLOTS, n + 1 + 6 * i)
                n0 = b0 + FB
                with pool.Fori(0, DT - 1) as m:
                    for c in range(3):
                        split_lo((n0 + c + 2) % SLOTS, n0 + c + 3 + 3 * m)
                n1 = n0 + 3 * (DT - 1)
                low(n1 + 2)
                if st + 1 < n_st:
                    hacc(st + 1, 0, range(0, 4))
                    low(n1 + 3)
                    hacc(st + 1, 0, range(4, 8))
                    low(n1 + 4)
                    low(n1 + 5)
                    hacc(st + 1, 1)

            def mix_out(st, n0):
                with pool.Fori(0, 2) as i:
                    for m in range(3):
                        split_lo((n0 + m + 2) % SLOTS, n0 + m + 3 + 3 * i)
                low(n0 + DT)
                hacc(st + 1, 0, range(0, 4))
                low(n0 + DT + 1)
                hacc(st + 1, 0, range(4, 8))
                low(n0 + DT + 2)
                hacc(st + 1, 1)

            def mla(st):
                n0 = first_block[st]
                for j in range(3, MLA_BLOCKS - DT + 2):
                    low(n0 + j)
                load_pages(pool, first_unit[st], s_cache_p, SP_PAGES, 4)
                mix_out(st, n0 + MLA_BLOCKS - DT)

            def gla(st):
                n0 = first_block[st]

                def k_mul(i):
                    if i < N_X:
                        hd, lv = x_of(i)
                        pool.wait_ge(g_exp, i + 1)
                        first = halves(xl[i % 3], lv)[0]
                        pool.tensor_tensor(first, first, halves(qk[:, GH + hd, :], lv)[0], ALU.mult).then_inc(g_xk, 1)

                low(n0 + 3)
                xi = n_a = n_s = 0
                for (kind, a, c), u in zip(g_plan, g_unit):
                    if kind == "in":
                        low(n0 + a + 2)
                    if kind == "kt" and a == TT - 1:
                        k_mul(0)
                        k_mul(1)
                    if kind == "lev":
                        if c < LEVELS:
                            k_mul(xi + 2)
                            xi += 1
                        if c > 0:
                            pool.wait_ge(s_evicted, first_unit[st] + u + 1)
                            if c > 1:
                                pool.wait_ge(g_att, n_a)
                            pool.tensor_tensor(att_p[:, a, :], att_p[:, a, :], masked[:, n_a % 2, :], ALU.add).then_inc(g_att, 1)
                            n_a += 1
                    if kind == "levs" and c > 4:
                        pool.wait_ge(s_evicted, first_unit[st] + u + 1)
                        if c > 5:
                            pool.wait_ge(g_att_s, n_s)
                        pool.tensor_tensor(att_s[:, a, :], att_s[:, a, :], masked_s[:, n_s % 2, :], ALU.add).then_inc(g_att_s, 1)
                        n_s += 1
                pool.wait_ge(s_evicted, first_unit[st] + G_SUM)
                for hd in range(GH):
                    for b in range(DEC_BATCH):
                        last = pool.tensor_scalar(k_own[:, hd, b, :], kd_t[0:NEW, QB, hd * DK:(hd + 1) * DK],
                                                  g_norm[0:NEW, DV // P + b:DV // P + b + 1], None, ALU.mult)
                    last.then_inc(g_own, 1)
                mix_out(st, n0 + GLA_IN)

            low(0)
            low(1)
            hacc(0, 0)
            low(2)
            hacc(0, 1)
            for st, kind in enumerate(stages):
                {"ffn": ffn, "mla": mla, "gla": gla}[kind](st)

        @blk.vector
        def _(dve):
            dve.memset(ones[:, :], 1.0)
            dve.memset(eps_d[:, :], EPS * D_MODEL)
            dve.memset(eps_q[:, :], EPS * Q_LORA)
            dve.memset(eps_kv[:, :], EPS * KV_LORA)
            dve.memset(one_c[:, :], 1.0)
            dve.wait_ge(s_const, 32)
            dve.tensor_scalar(gain_s[:, :], gains[:, :], float(D_MODEL) ** 0.5, None, ALU.mult).then_inc(s_gain, 1)
            dve.wait_ge(s_gain, 1)
            for r in (1, 5, 7, 11):
                sl = slice(r * DT, (r + 1) * DT)
                last = dve.tensor_scalar(gain_s[:, sl], gain_s[:, sl], FFN_RESID, None, ALU.mult)
            last.then_inc(s_gain, 1)

            def x_low(b, hf, k):
                dve.wait_ge(s_xhi, 2 * DT * b + DT * hf + k + 1)
                gk = pre_gain[b] * DT + k
                dve.scalar_tensor_tensor(out=x_lo[:, k, H[hf]], in0=h[:, k, H[hf]], scalar=gain_s[:, gk:gk + 1],
                                         in1=x_hi[:, k, H[hf]].bitcast(F32), op0=ALU.mult,
                                         op1=ALU.subtract).then_inc(s_xlo, 1)

            def post(b, hf, y):
                rst = work[:, 2 + hf, :]
                dve.wait_ge(s_root, stat_post[b] + hf + 1)
                dve.reciprocal(rst, rst).then_inc(s_rst, 1)
                dve.wait_ge(s_rst, 2 * (b - 1) + hf + 1)
                for k in range(DT + 2):
                    if k < DT:
                        gk = post_gain[b] * DT + k
                        dve.scalar_tensor_tensor(out=y[:, k, H[hf]], in0=y[:, k, H[hf]], scalar=gain_s[:, gk:gk + 1],
                                                 in1=rst, op0=ALU.mult, op1=ALU.mult).then_inc(s_yn, 1)
                    if 1 <= k <= DT:
                        dve.wait_ge(s_yn, 2 * DT * (b - 1) + DT * hf + k)
                        dve.tensor_tensor(h[:, k - 1, H[hf]], h[:, k - 1, H[hf]], y[:, k - 1, H[hf]],
                                          ALU.add).then_inc(s_hnew, 1)
                    if k >= 2 and b < n_st:
                        x_low(b, hf, k - 2)

            def evict(u, dst, hf, bk, r=P):
                dve.wait_ge(s_unit, u + 1)
                dve.tensor_tensor(dst, bank[bk][0:r, 0:HALF], r_pre[0:r, H[hf]], ALU.mult).then_inc(s_evicted, 1)

            def r_ready(b, hf):
                dve.wait_ge(s_root, stat_pre[b] + hf + 1)
                dve.reciprocal(r_pre[:, H[hf]], r_pre[:, H[hf]]).then_inc(s_rpre, 1)
                dve.wait_ge(s_rpre, 2 * b + hf + 1)

            def out_unit(st, y, m, hf, u, bk, sq_n, acc_n):
                dve.wait_ge(s_unit, u + 1)
                dve.tensor_copy(y[:, m, H[hf]], bank[bk][:, 0:HALF]).then_inc(s_evicted, 1)
                dve.wait_ge(s_sq, sq_n)
                if acc_n is None:
                    dve.tensor_copy(acc[:, H[hf]], work[:, hf, :]).then_inc(s_acc, 1)
                else:
                    dve.wait_ge(s_acc, acc_n)
                    dve.tensor_tensor(acc[:, H[hf]], acc[:, H[hf]], work[:, hf, :], ALU.add).then_inc(s_acc, 1)

            def gate_up(q, hf, ev):
                dve.wait_ge(s_silu, q + 1)
                dve.wait_ge(s_evicted, ev)
                dve.tensor_tensor(work[:, 2 + hf, :], work[:, hf, :], work[:, 2 + hf, :], ALU.mult).then_inc(s_gu, 1)

            def gate_low(q, hf, pi):
                dve.wait_ge(s_guhi, q + 1)
                dve.tensor_tensor(gu_lo[:, pi, H[hf]], work[:, 2 + hf, :], gu_hi[:, pi, H[hf]].bitcast(F32),
                                  ALU.subtract).then_inc(s_gulo, 1)

            def ffn(st):
                u0, f = first_unit[st], ffn_no[st]
                q0 = 2 * FT * f
                for hf in range(2):
                    r_ready(st, hf)
                    evict(u0 + 2 * hf, work[:, hf, :], hf, (u0 + 2 * hf) % RING)
                    evict(u0 + 2 * hf + 1, work[:, 2 + hf, :], hf, (u0 + 2 * hf + 1) % RING)
                    gate_up(q0 + hf, hf, u0 + 2 * hf + 2)
                for hf in range(2):
                    gate_low(q0 + hf, hf, 0)
                with dve.Fori(0, (FT - 1) // 3) as i:
                    for p in range(1, 4):
                        u = u0 + 4 * p
                        q = q0 + 2 * p
                        for hf in range(2):
                            evict(u + hf + 12 * i, work[:, hf, :], hf, (u + hf) % RING)
                        for hf in range(2):
                            dve.wait_ge(s_gulo, q + hf - 1 + 6 * i)
                            evict(u + 2 + hf + 12 * i, work[:, 2 + hf, :], hf, (u + 2 + hf) % RING)
                            gate_up(q + hf + 6 * i, hf, u + 3 + hf + 12 * i)
                            if hf == 1:
                                gate_low(q + 6 * i, 0, p + 3 * i)
                        gate_low(q + 1 + 6 * i, 1, p + 3 * i)
                v0, a0 = u0 + 4 * FT, 2 * DT * st
                for hf in range(2):
                    out_unit(st, y_ffn, 0, hf, v0 + hf, (v0 + hf) % RING, a0 + hf + 1, None)
                with dve.Fori(0, 2) as i:
                    for m in range(1, 4):
                        for hf in range(2):
                            n = 2 * m + hf + 6 * i
                            out_unit(st, y_ffn, m + 3 * i, hf, v0 + n, (v0 + 2 * m + hf) % RING, a0 + n + 1, a0 + n - 1)
                for hf in range(2):
                    n = 2 * DT - 2 + hf
                    out_unit(st, y_ffn, DT - 1, hf, v0 + n, (v0 + n) % RING, a0 + n + 1, a0 + n - 1)
                    post(st + 1, hf, y_ffn)

            def mix_out(st, v0):
                a0 = 2 * DT * st
                for hf in range(2):
                    out_unit(st, y_mix, 0, hf, v0 + hf, (v0 + hf) % RING, a0 + hf + 1, None)
                for m in range(1, 6):
                    for hf in range(2):
                        n = 2 * m + hf
                        out_unit(st, y_mix, m, hf, v0 + n, (v0 + n) % RING, a0 + n + 1, a0 + n - 1)
                for hf in range(2):
                    for j in range(2):
                        n = 12 + 2 * hf + j
                        before = a0 + n if j else a0 + 11 + hf
                        out_unit(st, y_mix, 6 + j, hf, v0 + n, (v0 + n) % RING, a0 + n + 1, before)
                    post(st + 1, hf, y_mix)

            def mla(st):
                u0 = first_unit[st]
                for hf in range(2):
                    r_ready(st, hf)
                    for j in range(2):
                        u = u0 + pair_unit(j, hf)
                        evict(u, down[:, j, H[hf]], hf, u % RING)
                for j in range(2, MLA_IN):
                    for hf in range(2):
                        u = u0 + pair_unit(j, hf)
                        evict(u, down[:, j, H[hf]], hf, u % RING)
                dve.wait_ge(s_mla_c, 48)
                dve.wait_ge(s_evicted, u0 + 2 * MLA_IN)
                t_k = [work[0:ROPE, 2 * i:2 * i + 2, :].rearrange("p a b -> p (a b)") for i in range(2)]
                dve.tensor_tensor(t_k[0], down[0:ROPE, MLA_IN - 1, :], rope_tab[0:ROPE, :], ALU.mult).then_inc(s_rt, 1)
                dve.tensor_tensor(t_k[1], down[ROPE:P, MLA_IN - 1, :], rope_tab[ROPE:P, :], ALU.mult).then_inc(s_rt, 1)
                dve.tensor_scalar(mla_g[:, 0:QT], mla_g[:, 0:QT], float(Q_LORA) ** 0.5, None, ALU.mult).then_inc(s_mg, 1)
                dve.tensor_scalar(mla_g[:, QT:], mla_g[:, QT:], float(KV_LORA) ** 0.5, None, ALU.mult).then_inc(s_mg, 1)
                dve.wait_ge(s_rt, 2)
                dve.tensor_tensor(kpe[:, :], t_k[0], t_k[1], ALU.add).then_inc(s_kpe, 1)
                for j in range(2):
                    for hf in range(2):
                        dst = (r_q, r_kv)[j][:, H[hf]]
                        dve.wait_ge(s_mroot, 2 * j + hf + 1)
                        dve.reciprocal(dst, dst).then_inc(s_evicted, 1)
                dve.wait_ge(s_mg, 2)
                dve.wait_ge(s_evicted, u0 + M_SUM + 4)
                for j in range(QT):
                    dve.scalar_tensor_tensor(out=down[:, j, :], in0=down[:, j, :], scalar=mla_g[:, j:j + 1],
                                             in1=r_q[:, :], op0=ALU.mult, op1=ALU.mult).then_inc(s_cq, 1)
                for j in range(KT):
                    dve.scalar_tensor_tensor(out=ckv[:, j, :], in0=down[:, QT + j, :], scalar=mla_g[:, QT + j:QT + j + 1],
                                             in1=r_kv[:, :], op0=ALU.mult, op1=ALU.mult).then_inc(s_ckv, 1)
                for j in range(QT):
                    dve.wait_ge(s_cqhi, j + 1)
                    dve.tensor_tensor(cq_lo[:, j, :], down[:, j, :], cq_hi[:, j, :].bitcast(F32),
                                      ALU.subtract).then_inc(s_cqlo, 1)
                for j in range(KT):
                    dve.wait_ge(s_kvhi, j + 1)
                    dve.tensor_tensor(kv_lo[:, j, :], ckv[:, j, :], kv_hi[:, j, :].bitcast(F32),
                                      ALU.subtract).then_inc(s_kvlo, 1)
                r = 0
                for hd in range(HEADS):
                    u = u0 + M_Q + 4 * hd
                    for hf in range(2):
                        dve.wait_ge(s_unit, u + hf + 1)
                        dve.tensor_copy(qn[:, hd, H[hf]], bank[(u + hf) % RING][:, 0:HALF]).then_inc(s_evicted, 1)
                    for hf in range(2):
                        ps = bank[(u + 2 + hf) % RING]
                        ta, tb = work[0:ROPE, 2 * hf, :], work[0:ROPE, 2 * hf + 1, :]
                        dve.wait_ge(s_unit, u + 2 + hf + 1)
                        dve.wait_ge(s_kpe, 1)
                        if r >= 2:
                            dve.wait_ge(s_rope, r - 1)
                        dve.tensor_tensor(ta, ps[0:ROPE, 0:HALF], rope_tab[0:ROPE, H[hf]], ALU.mult).then_inc(s_rt, 1)
                        dve.tensor_tensor(tb, ps[ROPE:P, 0:HALF], rope_tab[ROPE:P, H[hf]], ALU.mult).then_inc(s_evicted, 1)
                        dve.wait_ge(s_rt, 2 + r + 1)
                        dve.wait_ge(s_evicted, u + 2 + hf + 1)
                        dve.tensor_tensor(qpe[:, hd, H[hf]], ta, tb, ALU.add).then_inc(s_rope, 1)
                        r += 1
                for hd in range(HEADS):
                    u = u0 + M_K + hd
                    dve.wait_ge(s_unit, u + 1)
                    dve.tensor_copy(kn[:, hd, :], bank[u % RING]).then_inc(s_evicted, 1)
                for b in range(2):
                    for t in range(QB):
                        u = u0 + M_V + QB * b + t
                        dve.wait_ge(s_unit, u + 1)
                        dve.tensor_copy(vp[:, t, b * 512:(b + 1) * 512], bank[u % RING]).then_inc(s_evicted, 1)
                dve.wait_ge(s_rope, 2 * HEADS)
                for hd in range(HEADS):
                    dve.tensor_copy(q_pes[:, :, hd * DEC_SEQ:(hd + 1) * DEC_SEQ],
                                    qpe[:, hd, SEQ:TOK].rearrange("p (b t) -> p b t", t=DEC_SEQ)).then_inc(s_qpes, 1)
                for rt in range(KT):
                    u = u0 + M_L + rt
                    dve.wait_ge(s_unit, u + 1)
                    for hd in range(HEADS):
                        last = dve.tensor_copy(q_lat[:, rt, :, hd * DEC_SEQ:(hd + 1) * DEC_SEQ],
                                               bank[u % RING][:, hd * NEW:(hd + 1) * NEW].rearrange(
                                                   "p (b t) -> p b t", t=DEC_SEQ))
                    last.then_inc(s_evicted, 1)
                dve.wait_ge(s_evicted, u0 + M_O)
                dve.memset(soft[:, 4:8, :], 0.0).then_inc(s_rope, 1)

                def out_low(hd):
                    dve.wait_ge(s_ohi, hd + 1)
                    dve.tensor_tensor(x_lo[:, hd, 0:SEQ], bank[4 + hd % 2], x_hi[:, hd, 0:SEQ].bitcast(F32),
                                      ALU.subtract).then_inc(s_olo, 1)

                for w in range(ATT + 1):
                    if w < ATT:
                        i = w % QB
                        n = (i + 1) * P
                        dve.wait_ge(s_s, w + 1)
                        sc = bank[S_BANK[w % LOOK]]
                        dve.tensor_tensor(sc[:, i * P:n], sc[:, i * P:n], mask[:, 0:P],
                                          ALU.add).then_inc(s_msk, 1)
                        dve.wait_ge(s_msk, w + 1)
                        dve.tensor_reduce(soft[:, 0, w:w + 1], sc[:, 0:n], AX.X, ALU.max).then_inc(s_max, 1)
                        dve.wait_ge(s_max, w + 1)
                        dve.tensor_scalar(soft[:, 1, w:w + 1], soft[:, 0, w:w + 1], -MLA_SCALE, None,
                                          ALU.mult).then_inc(s_neg, 1)
                    if w >= 1:
                        n = ((w - 1) % QB + 1) * P
                        dve.wait_ge(s_exp, w)
                        dve.reciprocal(soft[:, 3, w - 1:w], soft[:, 2, w - 1:w]).then_inc(s_rec, 1)
                        dve.wait_ge(s_rec, w)
                        pr = prob[:, (w - 1) % LOOK, 0:n]
                        dve.tensor_scalar(pr, pr, soft[:, 3, w - 1:w], None, ALU.mult).then_inc(s_pn, 1)
                    if w % QB == 0 and w >= 2 * QB:
                        out_low(w // QB - 2)
                out_low(HEADS - 1)

                def pages(x):
                    dve.wait_ge(s_tr, 3 * x + 1)
                    if x >= 2:
                        dve.wait_ge(s_score, x - 1)
                    dve.tensor_copy(c_t[x % 2][:, 0, :], bank[4]).then_inc(s_ctv, 1)

                pages(0)
                for bp in range(PAIRS):
                    w, m0 = ATT + bp, 12 * bp
                    x0, x1 = 2 * GROUPS * bp, 2 * GROUPS * (bp + 1)
                    for x in range(x0, x1):
                        if x + 1 < x1:
                            pages(x + 1)
                        if x == x0 + 1:
                            dve.wait_ge(s_snew, 2 * (bp + 1))
                            dve.tensor_tensor(p_new[:, :], bank[7][:, 0:DEC_SEQ], mask[:, P:P + DEC_SEQ],
                                              ALU.add).then_inc(s_mxs, 1)
                            dve.wait_ge(s_mxs, m0 + 2)
                            dve.tensor_reduce(mx[:, bp, GROUPS:GROUPS + 1], p_new[:, :], AX.X, ALU.max).then_inc(s_mxs, 1)
                        e, g = slice(QR * (x // GROUPS % 2), QR * (x // GROUPS % 2) + QR), x % GROUPS
                        dve.wait_ge(s_score, x + 1)
                        dve.tensor_reduce(mx[e, bp, g:g + 1], psum[e, g, :], AX.X, ALU.max).then_inc(s_mxs, 1)
                    dve.wait_ge(s_mxs, m0 + 10)
                    dve.tensor_reduce(soft[:, 0, w:w + 1], mx[:, bp, :], AX.X, ALU.max).then_inc(s_mxs, 1)
                    dve.wait_ge(s_mxs, m0 + 11)
                    dve.tensor_scalar(soft[:, 1, w:w + 1], soft[:, 0, w:w + 1], -MLA_SCALE, None,
                                      ALU.mult).then_inc(s_negs, 1)
                    if bp + 1 < PAIRS:
                        pages(x1)
                    dve.wait_ge(s_fill, 6 * bp + 1)
                    dve.tensor_copy(rows[:, 0, :], bank[5][0:DEC_SEQ, P:P + KV_LORA])
                    dve.tensor_copy(rows[:, 1, :], bank[6][0:DEC_SEQ, 0:KV_LORA]).then_inc(s_fe, 1)
                    for f in (0, 2):
                        dve.wait_ge(s_fill, 6 * bp + 2 + f)
                        if bp > 0 and f == 0:
                            dve.wait_ge(s_pv, 2 * bp)
                        dve.tensor_copy(pt_s[:, 4 * f:4 * f + 4, :],
                                        bank[f].rearrange("p (g q) -> p g q", q=P)).then_inc(s_fe, 1)
                    dve.wait_ge(s_fill, 6 * bp + 6)
                    dve.tensor_copy(p_new_t[:, :], bank[5][0:DEC_SEQ, 0:P]).then_inc(s_fe, 1)
                    dve.wait_ge(s_exps, (GROUPS + 1) * (bp + 1))
                    dve.tensor_reduce(soft[:, 6, w:w + 1], sums[:, bp, :], AX.X, ALU.add).then_inc(s_mxs, 1)
                    dve.wait_ge(s_mxs, m0 + 12)
                    dve.reciprocal(soft[:, 7, w:w + 1], soft[:, 6, w:w + 1]).then_inc(s_recs, 1)
                    dve.wait_ge(s_recs, bp + 1)
                    dve.wait_ge(s_pv, 2 * (bp + 1))
                    dve.tensor_scalar(o_q[:, bp, :], bank[7][:, 8:8 + KV_LORA], soft[:, 7, w:w + 1], None,
                                      ALU.mult).then_inc(s_ole, 1)
                for rt in range(KT):
                    dve.wait_ge(s_fill, 6 * PAIRS + rt + 1)
                    dve.tensor_copy(o_lat[:, rt, :, :].rearrange("p b q -> p (b q)"), bank[rt]).then_inc(s_ole, 1)
                dve.wait_ge(s_ohi, HEADS + 1)
                dve.tensor_tensor(x_lo[:, :, SEQ:TOK], bank[4].rearrange("p (h q) -> p h q", h=HEADS),
                                  x_hi[:, :, SEQ:TOK].bitcast(F32), ALU.subtract).then_inc(s_olo, 1)
                mix_out(st, u0 + M_O)

            def gla(st):
                u0 = first_unit[st]
                dve.wait_ge(g_const, 48)
                dve.memset(eps_v[:, :], EPS * DV)
                dve.tensor_scalar(g_norm[:, 0:DV // P], g_norm[:, 0:DV // P], float(DV) ** 0.5, None,
                                  ALU.mult).then_inc(g_gain, 1)

                def in_evict(j, hf, u):
                    bk = bank[u % RING]
                    if j == 0:
                        evict(u, z_t[0:GATE_ONE, H[hf]], hf, u % RING, GATE_ONE)
                    elif j <= GH:
                        dve.wait_ge(s_unit, u + 1)
                        dve.scalar_tensor_tensor(out=qk[:, j - 1, H[hf]], in0=bk[:, 0:HALF], scalar=float(DK) ** -0.5,
                                                 in1=r_pre[:, H[hf]], op0=ALU.mult, op1=ALU.mult).then_inc(s_evicted, 1)
                    elif j <= 2 * GH:
                        evict(u, qk[:, j - 1, H[hf]], hf, u % RING)
                    else:
                        m = j - 1 - 2 * GH
                        evict(u, (vt_f if m < DT else og)[:, m % DT, H[hf]], hf, u % RING)

                def level_dif(i):
                    if i < N_X:
                        hd, lv = x_of(i)
                        x1, x2, _ = halves(xl[i % 3], lv)
                        g1, g2, ref = halves(cum[:, hd, :], lv)
                        if i >= 3:
                            dve.wait_ge(s_unit, u0 + lev_unit[i - 3] + 1)
                        dve.tensor_tensor(x1, ref, g1, ALU.subtract).then_inc(g_dif, 1)
                        dve.tensor_tensor(x2, g2, ref, ALU.subtract).then_inc(g_dif, 1)

                def q_mul(i):
                    if i < N_X:
                        hd, lv = x_of(i)
                        dve.wait_ge(g_exp, i + 1)
                        second = halves(xl[i % 3], lv)[1]
                        dve.tensor_tensor(second, second, halves(qk[:, hd, :], lv)[1], ALU.mult).then_inc(g_xq, 1)

                for hf in range(2):
                    r_ready(st, hf)
                    if hf == 0:
                        dve.wait_ge(s_hacc, 2 * DT * (st + 1))
                        dve.memset(z_t[GATE_ONE:GATE_ONE + 1, :], 1.0).then_inc(g_gain, 1)
                    for j in range(2):
                        u = u0 + pair_unit(j, hf)
                        in_evict(j, hf, u)
                xi = 0
                for (kind, a, c), un in zip(g_plan, g_unit):
                    u = u0 + un
                    bk = bank[u % RING]
                    if kind == "in":
                        for hf in range(2):
                            in_evict(a, hf, u + hf)
                    if kind in ("gate", "cum", "kt", "lev", "levs", "vt"):
                        dve.wait_ge(s_unit, u + 1)
                    if kind == "gate":
                        r = rows_of(a)
                        if a >= 2:
                            dve.wait_ge(g_gate, a - 1)
                        dve.tensor_copy(zc[0:r, a % 2, :], bk[0:r, :]).then_inc(s_evicted, 1)
                        dve.wait_ge(s_evicted, u + 1)
                        dve.scalar_tensor_tensor(out=gate[0:r, a, :], in0=zc[0:r, a % 2, :], scalar=-1.0,
                                                 in1=zc[0:r, a % 2, :], op0=ALU.mult, op1=ALU.max).then_inc(g_abs, 1)
                        dve.tensor_scalar(zmin[0:r, a, :], zc[0:r, a % 2, :], 0.0, None, ALU.min).then_inc(g_gate, 1)
                    if kind == "gate" and a == TT - 1:
                        for t in range(TT):
                            r = rows_of(t)
                            dve.wait_ge(g_ln, t + 1)
                            dve.wait_ge(g_gate, t + 1)
                            dve.tensor_tensor(gate[0:r, t, :], zmin[0:r, t, :], gate[0:r, t, :],
                                              ALU.subtract).then_inc(g_gate, 1)
                    if kind == "cum":
                        if a < GH:
                            dve.tensor_copy(cum[:, a, 0:SEQ], bk).then_inc(s_evicted, 1)
                        else:
                            dve.tensor_copy(cum[:, :, SEQ:], bk[:, 0:GH * NEW].rearrange("p (h q) -> p h q", h=GH)
                                            ).then_inc(s_evicted, 1)
                    if kind == "in" and a == 9:
                        dve.wait_ge(s_evicted, u)
                        for hd in range(GH):
                            dve.wait_ge(g_eg, TT + hd + 1)
                            dve.tensor_tensor(qg[:, hd, :], qg[:, hd, :], qk[:, hd, :], ALU.mult).then_inc(g_qg, 1)
                            for lo, hi, n in ((0, SEQ, P), (SEQ, TOK, DEC_SEQ)):
                                g = cum[:, hd, lo:hi].rearrange("p (c t) -> p c t", t=n)
                                d = kd[:, hd, lo:hi].rearrange("p (c t) -> p c t", t=n)
                                ref = g[:, :, n - 1:n].to_broadcast([P, (hi - lo) // n, n])
                                dve.tensor_tensor(d, ref, g, ALU.subtract).then_inc(g_kdif, 1)
                        for hd in range(GH):
                            dve.wait_ge(g_kexp, hd + 1)
                            dve.tensor_tensor(kd[:, hd, :], kd[:, hd, :], qk[:, GH + hd, :], ALU.mult).then_inc(g_kd, 1)
                    if kind == "kt":
                        r = rows_of(a)
                        dve.tensor_copy(kd_t[0:r, a, :], bk[0:r, :]).then_inc(s_evicted, 1)
                        if a == TT - 1:
                            for i in range(2):
                                level_dif(i)
                                q_mul(i)
                    if kind == "lev":
                        if c < LEVELS:
                            level_dif(xi + 2)
                        m = lmask[:, c:c + 1, :].to_broadcast([P, QB, P])
                        if c == 0:
                            dst = att_p[:, a, :]
                        else:
                            n_p = LEVELS * a + c - 1
                            dst = masked[:, n_p % 2, :]
                            if n_p >= 2:
                                dve.wait_ge(g_att, n_p - 1)
                        dve.tensor_tensor(dst.rearrange("p (c t) -> p c t", t=P), bk.rearrange("p (c t) -> p c t", t=P), m,
                                          ALU.mult).then_inc(s_evicted, 1)
                        if c < LEVELS:
                            q_mul(xi + 2)
                            xi += 1
                    if kind == "levs":
                        if c == 4:
                            dst = att_s[:, a, :]
                        else:
                            n_p = 3 * a + c - 5
                            dst = masked_s[:, n_p % 2, :]
                            if n_p >= 2:
                                dve.wait_ge(g_att_s, n_p - 1)
                        dve.tensor_tensor(dst, bk[0:NEW, 0:NEW], lmask[0:NEW, c, 0:NEW], ALU.mult).then_inc(s_evicted, 1)
                    if kind == "vt":
                        r = rows_of(a)
                        dve.tensor_copy(v_t[0:r, a, c * 512:(c + 1) * 512], bk[0:r, :]).then_inc(s_evicted, 1)
                for t in range(QB):
                    for hd in range(GH):
                        w = GH * t + hd
                        dve.wait_ge(g_o, w + 1)
                        dve.tensor_copy(o_t[:, 2 * hd:2 * hd + 2, t * P:(t + 1) * P],
                                        bank[w % 2][:, 0:2 * P].rearrange("p (j t) -> p j t", j=2)).then_inc(g_oe, 1)
                        dve.wait_ge(g_s, w + 1)
                        new = state[(t + 1) % 2][:, hd, :]
                        if t == 0:
                            dve.tensor_copy(new, bank[2 + w % 2][:, 0:DV]).then_inc(g_se, 1)
                        else:
                            dve.wait_ge(g_last, 2)
                            dve.wait_ge(g_se, w - GH + 1)
                            dve.scalar_tensor_tensor(out=new, in0=state[t % 2][:, hd, :], scalar=glast[:, hd, t:t + 1],
                                                     in1=bank[2 + w % 2][:, 0:DV], op0=ALU.mult,
                                                     op1=ALU.add).then_inc(g_se, 1)
                for b in range(DEC_BATCH):
                    for p in range(2):
                        dve.wait_ge(g_sn, 2 * b + p + 1)
                        for i in range(2):
                            hd = 2 * p + i
                            s_b = st_s[b % SS][:, hd, :]
                            last = dve.scalar_tensor_tensor(out=s_b, in0=s_b, scalar=glast[:, hd, QB + b:QB + b + 1],
                                                            in1=bank[6 + p][:, i * DV:(i + 1) * DV],
                                                            op0=ALU.mult, op1=ALU.add)
                        last.then_inc(g_sne, 1)
                dve.wait_ge(g_so, 1)
                dve.tensor_copy(o_t[:, :, SEQ:], bank[4].rearrange("p (j t) -> p j t", j=DT)).then_inc(g_soe, 1)
                for hd in range(GH):
                    for hf in range(2):
                        dve.wait_ge(g_root, 2 * hd + hf + 1)
                        dve.reciprocal(o_r[:, hd, H[hf]], o_r[:, hd, H[hf]]).then_inc(s_evicted, 1)
                dve.wait_ge(s_evicted, u0 + G_O)
                dve.wait_ge(g_osq, DT)
                for m in range(DT):
                    dve.scalar_tensor_tensor(out=o_t[:, m, :], in0=o_t[:, m, :], scalar=g_norm[:, m % 2:m % 2 + 1],
                                             in1=o_r[:, m // 2, :], op0=ALU.mult, op1=ALU.mult).then_inc(g_on, 1)
                for m in range(DT):
                    dve.wait_ge(g_on, m + 1)
                    dve.wait_ge(g_silu, m + 1)
                    dve.tensor_tensor(o_t[:, m, :], o_t[:, m, :], og[:, m, :], ALU.mult).then_inc(g_og, 1)
                for m in range(DT):
                    dve.wait_ge(g_ohi, m + 1)
                    dve.tensor_tensor(x_lo[:, m, :], o_t[:, m, :], x_hi[:, m, :].bitcast(F32),
                                      ALU.subtract).then_inc(g_olo, 1)
                for i in range(SS):
                    dve.wait_ge(g_store[i], 32 if i + SS < DEC_BATCH else 16)
                mix_out(st, u0 + G_O)

            for hf in range(2):
                for k in range(DT):
                    x_low(0, hf, k)
            for st, kind in enumerate(stages):
                {"ffn": ffn, "mla": mla, "gla": gla}[kind](st)

        @blk.tensor
        def _(pe):
            def three(out, w, x, start, stop):
                (wh, wl), (xh, xl) = w, x
                pe.matmul(out, wh, xh, start=start, stop=False)
                pe.matmul(out, wh, xl, start=False, stop=False)
                return pe.matmul(out, wl, xh, start=False, stop=stop)

            def weights(slot, c0, n=P):
                return w_hi[slot][:, c0:c0 + n], w_lo[slot][:, c0:c0 + n]

            def free(u):
                if not (isinstance(u, int) and u < RING):
                    pe.wait_ge(s_evicted, u - (RING - 1))

            def free_soon(u):
                pe.wait_ge(s_evicted, u - (RING - 3))

            def x_unit(bk, slot, hf, wait_x=None):
                for k in range(DT):
                    if wait_x is not None:
                        pe.wait_ge(s_xlo, wait_x + k + 1)
                    last = three(bank[bk][:, 0:HALF], weights(slot, k * P), (x_hi[:, k, H[hf]], x_lo[:, k, H[hf]]),
                                 k == 0, k == DT - 1)
                return last

            def stat(hf):
                pe.matmul(bank[6 + hf][:, 0:HALF], ones[:, :], acc[:, H[hf]], start=True, stop=True).then_inc(s_stat, 1)

            def in_pair(st):
                b0, u0 = first_block[st], first_unit[st]
                for hf in range(2):
                    for j in range(2):
                        u = u0 + 2 * hf + j
                        if hf == 0:
                            pe.wait_ge(s_lo, b0 + j + 1)
                        free(u)
                        last = x_unit(u % RING, (b0 + j) % SLOTS, hf, 2 * DT * st + DT * hf if j == 0 else None)
                        last.then_inc(s_unit, 1)
                    pe.wait_ge(s_hacc, 2 * DT * st + DT * (hf + 1))
                    stat(hf)

            def ffn(st):
                b0, u0, f = first_block[st], first_unit[st], ffn_no[st]
                in_pair(st)
                with pe.Fori(0, (FT - 1) // 3) as i:
                    for p in range(1, 4):
                        for g in range(2):
                            n = b0 + 2 * p + g
                            pe.wait_ge(s_lo, n + 1 + 6 * i)
                            for hf in range(2):
                                u = u0 + 4 * p + 2 * g + hf
                                free_soon(u + 12 * i)
                                x_unit(u % RING, n % SLOTS, hf).then_inc(s_unit, 1)
                n0, v0 = b0 + FB, u0 + 4 * FT
                pe.wait_ge(s_gulo, 2 * FT * (f + 1))

                def out_part(c, hf, slot, bk):
                    k0 = sum(OUT_SPLIT[:c])
                    for k in range(OUT_SPLIT[c]):
                        last = three(bank[bk][:, 0:HALF], weights(slot, k * P),
                                     (gu_hi[:, k0 + k, H[hf]], gu_lo[:, k0 + k, H[hf]]),
                                     c == 0 and k == 0, c == len(OUT_SPLIT) - 1 and k == OUT_SPLIT[c] - 1)
                    return last

                def out_tile(m, more):
                    for c in range(3):
                        n = n0 + 3 * m + c
                        pe.wait_ge(s_lo, n + 1 + 3 * more)
                        for hf in range(2):
                            u = v0 + 2 * m + hf
                            if c == 0:
                                free(u + 2 * more)
                            last = out_part(c, hf, n % SLOTS, u % RING)
                            if c == 2:
                                last.then_inc(s_unit, 1)
                        if c < 2:
                            last.then_inc(s_used, 1)

                out_tile(0, 0)
                with pe.Fori(0, 2) as i:
                    for m in range(1, 4):
                        out_tile(m, 3 * i)
                n1, v1 = n0 + 3 * (DT - 1), v0 + 2 * (DT - 1)
                for hf in range(2):
                    free(v1 + hf)
                    for c in range(3):
                        if hf == 0:
                            pe.wait_ge(s_lo, n1 + c + 1)
                        last = out_part(c, hf, (n1 + c) % SLOTS, (v1 + hf) % RING)
                        if hf == 1:
                            if c < 2:
                                last.then_inc(s_used, 1)
                            if c == 0:
                                pe.wait_ge(s_acc, 2 * DT * (st + 1) - 1)
                                pe.wait_ge(s_rpre, 2 * st + 2)
                                stat(0)
                        if c == 2:
                            last.then_inc(s_unit, 1)
                pe.wait_ge(s_acc, 2 * DT * (st + 1))
                stat(1)

            def mix_out(st, n0, v0):
                for m in range(6):
                    pe.wait_ge(s_lo, n0 + m + 1)
                    for hf in range(2):
                        u = v0 + 2 * m + hf
                        free(u)
                        x_unit(u % RING, (n0 + m) % SLOTS, hf).then_inc(s_unit, 1)
                for hf in range(2):
                    for j in range(2):
                        u = v0 + 12 + 2 * hf + j
                        if hf == 0:
                            pe.wait_ge(s_lo, n0 + 6 + j + 1)
                        free(u)
                        x_unit(u % RING, (n0 + 6 + j) % SLOTS, hf).then_inc(s_unit, 1)
                        if hf == 1 and j == 0:
                            pe.wait_ge(s_acc, 2 * DT * st + 14)
                            pe.wait_ge(s_rpre, 2 * st + 2)
                            stat(0)
                pe.wait_ge(s_acc, 2 * DT * st + 16)
                stat(1)

            def mla(st):
                n0, u0 = first_block[st], first_unit[st]
                in_pair(st)
                for j in range(2, MLA_IN):
                    pe.wait_ge(s_lo, n0 + j + 1)
                    for hf in range(2):
                        u = u0 + pair_unit(j, hf)
                        free(u)
                        x_unit(u % RING, (n0 + j) % SLOTS, hf).then_inc(s_unit, 1)
                for lo, hi in ((0, QT), (QT, QT + KT)):
                    pe.wait_ge(s_dsq, hi)
                    for hf in range(2):
                        u = u0 + M_SUM + 2 * (lo > 0) + hf
                        free(u)
                        for j in range(lo, hi):
                            last = pe.matmul(bank[u % RING][:, 0:HALF], ones[:, :], down_sq[:, j, H[hf]],
                                             start=j == lo, stop=j == hi - 1)
                        last.then_inc(s_unit, 1)
                pe.wait_ge(s_cqlo, QT)
                for hd in range(HEADS):
                    n = n0 + MLA_IN + hd
                    pe.wait_ge(s_lo, n + 1)
                    for part in range(2):
                        for hf in range(2):
                            u = u0 + M_Q + 4 * hd + 2 * part + hf
                            free(u)
                            for k in range(QT):
                                last = three(bank[u % RING][:, 0:HALF], weights(n % SLOTS, (2 * k + part) * P),
                                             (cq_hi[:, k, H[hf]], cq_lo[:, k, H[hf]]), k == 0, k == QT - 1)
                            last.then_inc(s_unit, 1)
                pe.wait_ge(s_kvlo, KT)
                for hd in range(HEADS):
                    n = n0 + MLA_IN + HEADS + hd // 4
                    u = u0 + M_K + hd
                    pe.wait_ge(s_lo, n + 1)
                    free(u)
                    for k in range(KT):
                        last = three(bank[u % RING], weights(n % SLOTS, (4 * k + hd % 4) * P),
                                     (kv_hi[:, k, 0:SEQ], kv_lo[:, k, 0:SEQ]), k == 0, k == KT - 1)
                    last.then_inc(s_unit, 1)
                for b in range(2):
                    n = n0 + MLA_IN + HEADS + 2 + b
                    pe.wait_ge(s_lo, n + 1)
                    for t in range(QB):
                        u = u0 + M_V + QB * b + t
                        free(u)
                        for k in range(KT):
                            last = three(bank[u % RING], (kv_hi[:, k, t * P:(t + 1) * P], kv_lo[:, k, t * P:(t + 1) * P]),
                                         weights(n % SLOTS, k * 512, 512), k == 0, k == KT - 1)
                        last.then_inc(s_unit, 1)
                pe.wait_ge(s_ukt, 16)
                for rt in range(KT):
                    u = u0 + M_L + rt
                    free(u)
                    for hd in range(HEADS):
                        last = pe.matmul(bank[u % RING][:, hd * NEW:(hd + 1) * NEW], uk_t[:, hd, rt * P:(rt + 1) * P],
                                         qn[:, hd, SEQ:TOK], start=True, stop=True)
                    last.then_inc(s_unit, 1)
                pe.wait_ge(s_evicted, u0 + M_O)

                def scores(w):
                    hd, i = w // QB, w % QB
                    n = (i + 1) * P
                    out = bank[S_BANK[w % LOOK]][:, 0:n]
                    if w >= LOOK:
                        pe.wait_ge(s_exp, w - LOOK + 1)
                    pe.matmul(out, qn[:, hd, i * P:n], kn[:, hd, 0:n], start=True, stop=False)
                    pe.matmul(out, qpe[:, hd, i * P:n], kpe[:, 0:n], start=False, stop=True).then_inc(s_s, 1)

                def head_out(hd):
                    pe.wait_ge(s_pt, QB * (hd + 1))
                    if hd >= 2:
                        pe.wait_ge(s_olo, hd - 1)
                    for kt in range(QB):
                        last = pe.matmul(bank[4 + hd % 2][:, kt * P:SEQ], vp[:, kt, hd * VD:(hd + 1) * VD],
                                         pt[hd % 2][:, kt, kt * P:SEQ], start=kt == 0, stop=kt == QB - 1)
                    last.then_inc(s_o, 1)

                scores(0)
                scores(1)
                for w in range(ATT):
                    if w + 2 < ATT:
                        scores(w + 2)
                    pe.wait_ge(s_pn, w + 1)
                    if w >= 2:
                        pe.wait_ge(s_pt, w - 1)
                    for kt in range(w % QB + 1):
                        last = pe.transpose(bank[2 + w % 2][:, kt * P:(kt + 1) * P],
                                            prob[:, w % LOOK, kt * P:(kt + 1) * P], ident[:, :])
                    last.then_inc(s_t, 1)
                    if w % QB == 1 and w > QB:
                        head_out(w // QB - 1)
                head_out(HEADS - 1)
                pe.wait_ge(s_olo, HEADS)

                def transpose_pages(x):
                    b, g = x // GROUPS, x % GROUPS
                    pe.wait_ge(s_cache[b % SLOTS][g], 16 * SP_PAGES * (b // SLOTS + 1))
                    pe.wait_ge(s_cache_p[b % SLOTS][g], 16 * (4 - SP_PAGES) * (b // SLOTS + 1))
                    for j in range(3):
                        if x >= 1:
                            pe.wait_ge(*((s_ctv, x) if j == 0 else (s_cta, 2 * x - 2 + j)))
                        for p in range(4):
                            pg = 4 * g + p
                            if j < 2:
                                last = pe.transpose(bank[4 + j][:, p * P:(p + 1) * P],
                                                    cache[b % SLOTS][:, pg, j * P:(j + 1) * P], ident[:, :])
                            else:
                                last = pe.transpose(bank[6][0:ROPE, p * P:(p + 1) * P], cache[b % SLOTS][:, pg, KV_LORA:],
                                                    ident[:, :])
                        last.then_inc(s_tr, 1)

                def group_scores(x):
                    b, g = x // GROUPS, x % GROUPS
                    e = slice(QR * (b % 2), QR * (b % 2) + QR)
                    pe.wait_ge(s_ctv, x + 1)
                    pe.wait_ge(s_cta, 2 * (x + 1))
                    if b >= 2:
                        pe.wait_ge(s_exps, (GROUPS + 1) * (b // 2))
                    out = psum[e, g, :]
                    for rt in range(KT):
                        pe.matmul(out, q_lat[:, rt, b, :], c_t[x % 2][:, rt, :], start=rt == 0, stop=False)
                    pe.matmul(out, q_pes[:, b, :], c_t[x % 2][0:ROPE, 2, :], start=False, stop=True).then_inc(s_score, 1)

                def new_scores(b):
                    e = slice(QR * (b % 2), QR * (b % 2) + QR)
                    new = slice(SEQ + DEC_SEQ * b, SEQ + DEC_SEQ * (b + 1))
                    if b >= 2:
                        pe.wait_ge(s_ole, b // 2)
                    for rt in range(KT):
                        pe.matmul(psum[e, 7, 0:DEC_SEQ], q_lat[:, rt, b, :], ckv[:, rt, new], start=rt == 0, stop=False)
                    pe.matmul(psum[e, 7, 0:DEC_SEQ], q_pes[:, b, :], kpe[:, new], start=False,
                              stop=True).then_inc(s_snew, 1)

                transpose_pages(0)
                for bp in range(PAIRS):
                    x0, x1 = 2 * GROUPS * bp, 2 * GROUPS * (bp + 1)
                    for x in range(x0, x1):
                        if x + 1 < x1:
                            transpose_pages(x + 1)
                        if x == x0 + 1:
                            new_scores(2 * bp)
                            new_scores(2 * bp + 1)
                        group_scores(x)
                    if bp + 1 < PAIRS:
                        transpose_pages(x1)
                    done = min(x1 + 1, 2 * GROUPS * PAIRS)
                    pe.wait_ge(s_cta, 2 * done)
                    for e in range(2):
                        new = slice(SEQ + DEC_SEQ * (2 * bp + e), SEQ + DEC_SEQ * (2 * bp + e + 1))
                        for rt in range(KT):
                            c0 = P * (1 - e) + rt * P
                            last = pe.transpose(bank[5 + e][0:DEC_SEQ, c0:c0 + P], ckv[:, rt, new], ident[:, :])
                    last.then_inc(s_fill, 1)
                    for f in range(GROUPS):
                        pe.wait_ge(s_exps, (GROUPS + 1) * bp + f + 1)
                        for p in range(4):
                            last = pe.transpose(bank[f][:, p * P:(p + 1) * P], p_s[:, f, p * P:(p + 1) * P], ident[:, :])
                        last.then_inc(s_fill, 1)
                    pe.wait_ge(s_exps, (GROUPS + 1) * (bp + 1))
                    pe.wait_ge(s_fe, 4 * bp + 1)
                    pe.transpose(bank[5][0:DEC_SEQ, 0:P], p_new[:, :], ident[:, :]).then_inc(s_fill, 1)
                    for e in range(2):
                        b = 2 * bp + e
                        q = slice(QR * e, QR * e + QR)
                        out = psum[q, 7, 8:8 + KV_LORA]
                        for pg in range(PAGES):
                            if e == 0 and pg % 4 == 0:
                                f = pg // 4
                                if f % 2:
                                    pe.wait_ge(s_fa, 2 * bp + f // 2 + 1)
                                else:
                                    pe.wait_ge(s_fe, 4 * bp + 2 + f // 2)
                            pe.matmul(out, pt_s[:, pg, q], cache[b % SLOTS][:, pg, 0:KV_LORA], start=pg == 0, stop=False)
                        if e == 0:
                            pe.wait_ge(s_fe, 4 * bp + 4)
                        pe.matmul(out, p_new_t[:, q], rows[:, e, :], start=False, stop=True).then_inc(s_pv, 1)
                pe.wait_ge(s_ole, PAIRS)
                for rt in range(KT):
                    for bp in range(PAIRS):
                        last = pe.transpose(bank[rt][:, bp * P:(bp + 1) * P], o_q[:, bp, rt * P:(rt + 1) * P], ident[:, :])
                    last.then_inc(s_fill, 1)
                pe.wait_ge(s_uvf, 16)
                pe.wait_ge(s_ole, PAIRS + KT)
                for hd in range(HEADS):
                    for rt in range(KT):
                        last = pe.matmul(bank[4][:, hd * NEW:(hd + 1) * NEW], uv_f[:, rt, hd * VD:(hd + 1) * VD],
                                         o_lat[:, rt, :, hd * DEC_SEQ:(hd + 1) * DEC_SEQ],
                                         start=rt == 0, stop=rt == KT - 1)
                last.then_inc(s_so, 1)
                pe.wait_ge(s_olo, HEADS + 1)
                mix_out(st, n0 + MLA_BLOCKS - DT, u0 + M_O)

            def gla(st):
                n0, u0 = first_block[st], first_unit[st]
                in_pair(st)
                xi = 0
                for (kind, a, c), un in zip(g_plan, g_unit):
                    u = u0 + un
                    bk = bank[u % RING]
                    if kind == "in":
                        pe.wait_ge(s_lo, n0 + a + 1)
                        for hf in range(2):
                            free(u + hf)
                            x_unit((u + hf) % RING, (n0 + a) % SLOTS, hf).then_inc(s_unit, 1)
                        continue
                    free(u)
                    if kind == "gate":
                        r = rows_of(a)
                        pe.wait_ge(g_const, 64)
                        pe.wait_ge(g_gain, 2)
                        last = pe.matmul(bk[0:r, :], z_t[0:GATE_ONE + 1, a * P:a * P + r], gk2[:, :], start=True, stop=True)
                    elif kind == "cum":
                        pe.wait_ge(g_gate, 2 * TT)
                        for i in range(QB if a < GH else GH):
                            if a < GH:
                                last = pe.matmul(bk[:, i * P:(i + 1) * P], gate[:, i, a * DK:(a + 1) * DK], tri[:, 0:P],
                                                 start=True, stop=True)
                            else:
                                last = pe.matmul(bk[:, i * NEW:(i + 1) * NEW], gate[0:NEW, QB, i * DK:(i + 1) * DK],
                                                 tri[0:NEW, P:], start=True, stop=True)
                    elif kind == "kt":
                        r = rows_of(a)
                        pe.wait_ge(g_kd, GH)
                        for hd in range(GH):
                            last = pe.transpose(bk[0:r, hd * DK:(hd + 1) * DK], kd[:, hd, a * P:a * P + r], ident[:, :])
                    elif kind == "vt":
                        r = rows_of(a)
                        for i in range(4):
                            last = pe.transpose(bk[0:r, i * P:(i + 1) * P], vt_f[:, 4 * c + i, a * P:a * P + r], ident[:, :])
                    else:
                        if c < LEVELS:
                            x = LEVELS * a + c
                            left = right = xl[x % 3][:, :]
                            if kind == "lev":
                                pe.wait_ge(g_xq, x + 1)
                                pe.wait_ge(g_xk, x + 1)
                        else:
                            left, right = qk[:, GH + a, :], qk[:, a, :]
                        if kind == "lev":
                            for t in range(QB):
                                tl = slice(t * P, (t + 1) * P)
                                last = pe.matmul(bk[:, tl], left[:, tl], right[:, tl], start=True, stop=True)
                        else:
                            last = pe.matmul(bk[0:NEW, 0:NEW], left[:, SEQ:TOK], right[:, SEQ:TOK], start=True, stop=True)
                    last.then_inc(s_unit, 1)
                pe.wait_ge(s_evicted, u0 + G_SUM)
                pe.wait_ge(g_att, GH * LEVELS)
                pe.wait_ge(g_att_s, 3 * GH)
                for t in range(QB):
                    tl = slice(t * P, (t + 1) * P)
                    for hd in range(GH):
                        w = GH * t + hd
                        if w >= 2:
                            pe.wait_ge(g_oe, w - 1)
                            pe.wait_ge(g_se, w - 1)
                        if t > 0:
                            pe.wait_ge(g_se, w - GH + 1)
                        for j in range(2):
                            out = bank[w % 2][:, j * P:(j + 1) * P]
                            vj = slice(hd * DV + j * P, hd * DV + (j + 1) * P)
                            last = pe.matmul(out, v_t[:, t, vj], att_p[:, hd, tl], start=True, stop=t == 0)
                            if t > 0:
                                last = pe.matmul(out, state[t % 2][:, hd, j * P:(j + 1) * P], qg[:, hd, tl],
                                                 start=False, stop=True)
                        last.then_inc(g_o, 1)
                        pe.matmul(bank[2 + w % 2][:, 0:DV], kd_t[:, t, hd * DK:(hd + 1) * DK],
                                  v_t[:, t, hd * DV:(hd + 1) * DV], start=True, stop=True).then_inc(g_s, 1)
                for hd in range(GH):
                    for j in range(2):
                        c0 = (2 * hd + j) * NEW
                        pe.matmul(bank[4][:, c0:c0 + NEW], v_t[0:NEW, QB, hd * DV + j * P:hd * DV + (j + 1) * P],
                                  att_s[:, hd, :], start=hd == 0 and j == 0, stop=False, skip_group_check=True)
                pe.wait_ge(g_own, GH)
                for b in range(DEC_BATCH):
                    pe.wait_ge(g_load[b % SS], 16 * (b // SS + 1))
                    own = slice(SEQ + DEC_SEQ * b, SEQ + DEC_SEQ * (b + 1))
                    for hd in range(GH):
                        for j in range(2):
                            c0 = (2 * hd + j) * NEW + DEC_SEQ * b
                            last = pe.matmul(bank[4][:, c0:c0 + DEC_SEQ], st_s[b % SS][:, hd, j * P:(j + 1) * P],
                                             qg[:, hd, own], start=False, stop=b == DEC_BATCH - 1,
                                             skip_group_check=True)
                    if b == DEC_BATCH - 1:
                        last.then_inc(g_so, 1)
                    for p in range(2):
                        if b > 0:
                            pe.wait_ge(g_sne, 2 * (b - 1) + p + 1)
                        for i in range(2):
                            hd = 2 * p + i
                            last = pe.matmul(bank[6 + p][:, i * DV:(i + 1) * DV], k_own[:, hd, b, :],
                                             v_t[0:NEW, QB, hd * DV:(hd + 1) * DV], start=True, stop=True)
                        last.then_inc(g_sn, 1)
                pe.wait_ge(g_soe, 1)
                pe.wait_ge(g_osq, DT)
                for hd in range(GH):
                    for hf in range(2):
                        u = u0 + G_SUM + 2 * hd + hf
                        free(u)
                        for j in range(2):
                            last = pe.matmul(bank[u % RING][:, 0:HALF], ones[:, :], o_sq[:, 2 * hd + j, H[hf]],
                                             start=j == 0, stop=j == 1)
                        last.then_inc(s_unit, 1)
                pe.wait_ge(g_olo, DT)
                mix_out(st, n0 + GLA_IN, u0 + G_O)

            for st, kind in enumerate(stages):
                {"ffn": ffn, "mla": mla, "gla": gla}[kind](st)


def rotary_tables():
    half = ROPE // 2
    inv = (10000.0 ** (-np.arange(half) / half)).astype(np.float32)
    pos = np.concatenate([np.arange(SEQ), np.tile(PAST + np.arange(DEC_SEQ), DEC_BATCH)]).astype(np.float32)
    ang = inv[:, None] * pos[None, :]
    cos, sin = np.cos(ang), np.sin(ang)
    return np.concatenate([cos, cos, -sin, sin]).astype(np.float32)


def causal_masks():
    q, k = np.arange(P)[:, None], np.arange(P)[None, :]
    t, j = np.arange(P)[:, None] % DEC_SEQ, np.arange(DEC_SEQ)[None, :]
    return np.concatenate([np.where(k <= q, 0.0, -1e30), np.where(j <= t, 0.0, -1e30)], 1).astype(np.float32)


def lay_out(a):
    def tiles(w, cols):
        k, n = w.shape
        return w.reshape(k // P, P, n // cols, cols).transpose(2, 1, 0, 3)

    def flat(t):
        return np.ascontiguousarray(t.reshape(t.shape[0], P, -1))

    x = np.concatenate([a["x_prompt"].reshape(SEQ, D_MODEL), a["x_sample"].reshape(NEW, D_MODEL)])
    down, uq = a["mla_w_down"][0], a["mla_w_uq"][0].reshape(Q_LORA, HEADS, NOPE + ROPE)
    swap = np.r_[ROPE // 2:ROPE, 0:ROPE // 2]
    pe = down[:, Q_LORA + KV_LORA:]
    down = np.concatenate([down, pe[:, swap]], 1)
    uq = np.concatenate([uq, uq[:, :, NOPE + swap]], 2).reshape(Q_LORA, HEADS * 2 * P)
    uk, uv = a["mla_w_uk"][0], a["mla_w_uv"][0]
    ffn_in = a["ffn_w_in"].reshape(4, DT, P, 2, FT, P).transpose(0, 4, 3, 2, 1, 5).reshape(4, 2 * FT, P, DT * P)
    ffn_out = a["ffn_w_out"].reshape(4, FT, P, DT, P).transpose(0, 3, 2, 1, 4).reshape(4, DT, P, FT * P)
    out = {
        "x_t": x.T.reshape(DT, P, TOK).transpose(1, 0, 2),
        "gains": a["norm_g"].reshape(12, DT, P).transpose(2, 0, 1).reshape(P, 12 * DT),
        "ffn_in": ffn_in,
        "ffn_out": ffn_out,
        "mla_down": flat(tiles(down, P)),
        "mla_uq": flat(tiles(uq, 2 * P)),
        "mla_uk": flat(tiles(uk.reshape(KV_LORA, HEADS * NOPE), 512)),
        "mla_uv": flat(tiles(uv.reshape(KV_LORA, HEADS * VD), 512)),
        "mla_uk_t": uk.transpose(2, 1, 0),
        "mla_uv_f": uv.reshape(KT, P, HEADS * VD).transpose(1, 0, 2),
        "mla_wo": flat(tiles(a["mla_w_o"][0], P)),
        "mla_g": np.concatenate([a["mla_g_q"][0], a["mla_g_kv"][0]]).reshape(QT + KT, P).T,
        "cache": np.concatenate([a["cache_ckv"][0], a["cache_kpe"][0]], 2),
        "page_table": a["page_table"].reshape(1, -1),
        "ident": np.eye(P, dtype=np.float32),
        "rope_tab": rotary_tables(),
        "mask": causal_masks(),
    }
    out.update(gla_lay_out(a, tiles, flat))
    return {k: np.ascontiguousarray(v) for k, v in out.items()}


def gla_lay_out(a, tiles, flat):
    w_in = np.concatenate([a["gla_w_gk1"][0], np.zeros((D_MODEL, P - GATE_RANK), np.float32), a["gla_w_in"][0]], 1)
    gk2 = np.zeros((GATE_ONE + 1, GH * DK), np.float32)
    gk2[0:GATE_RANK], gk2[GATE_ONE] = a["gla_w_gk2"][0], a["gla_b_gk"][0]
    s, t = np.arange(P)[:, None], np.arange(P)[None, :]
    masks = []
    for lv in range(LEVELS):
        b = P >> (lv + 1)
        masks.append((s // (2 * b) == t // (2 * b)) & (s // b % 2 == 0) & (t // b % 2 == 1))
    masks.append(s == t)
    s8, t8 = s[:, :NEW], t[:, :NEW]
    tri = np.concatenate([s <= t, (s8 <= t8) & (s8 // DEC_SEQ == t8 // DEC_SEQ)], 1) / GATE_NORM
    own = s // DEC_SEQ == np.arange(DEC_BATCH)[None, :]
    return {
        "gla_in": flat(tiles(w_in, P)),
        "gla_wo": flat(tiles(a["gla_w_o"][0], P)),
        "gk2": gk2,
        "lmask": np.stack(masks, 1).astype(np.float32),
        "tri": tri.astype(np.float32),
        "g_norm": np.concatenate([a["gla_g_norm"][0].reshape(DV // P, P).T, own], 1).astype(np.float32),
        "state_gla": a["state_gla"][0].transpose(0, 2, 1, 3),
    }


OUTPUTS = {"state_p": (P, GH, DV), "state_s": (DEC_BATCH, P, GH, DV), "y_t": (P, DT, TOK), "ckv_t": (P, KT, TOK), "kpe_t": (ROPE, TOK)}


def kernel(**inputs):
    import concourse.bacc as _bacc
    from concourse.bass_utils import run_bass_kernel_spmd as _run

    nc = _bacc.Bacc("TRN2", target_bir_lowering=False, num_devices=1)
    arrays = lay_out(inputs)
    io = {k: nc.dram_tensor(k, v.shape, mybir.dt.from_np(v.dtype), kind="ExternalInput").ap() for k, v in arrays.items()}
    for name, shape in OUTPUTS.items():
        io[name] = nc.dram_tensor(name, shape, F32, kind="ExternalOutput").ap()
    hybrid_step(nc, io)
    got = _run(nc, [arrays], core_ids=[0]).results[0]

    def by_token(t):
        return t.transpose(1, 0, 2).reshape(-1, TOK).T

    y, ckv, kpe = by_token(got["y_t"]), by_token(got["ckv_t"]), got["kpe_t"].T
    return (
        y[:SEQ].reshape(1, SEQ, D_MODEL),
        y[SEQ:].reshape(DEC_BATCH, DEC_SEQ, D_MODEL),
        ckv[:SEQ].reshape(1, 1, SEQ, KV_LORA),
        kpe[:SEQ].reshape(1, 1, SEQ, ROPE),
        ckv[SEQ:].reshape(1, DEC_BATCH, DEC_SEQ, KV_LORA),
        kpe[SEQ:].reshape(1, DEC_BATCH, DEC_SEQ, ROPE),
        got["state_p"].transpose(1, 0, 2)[None, None],
        got["state_s"].transpose(0, 2, 1, 3)[None],
    )
```
